# Optimizing a Trainium2 kernel written in Bass

```python
import math
import jax
import jax.numpy as jnp
from jax import lax
import numpy as np
import jax, jax.numpy as jnp

D_MODEL = 1024
BATCH = 1
SEQ = 512
DEPTH = 1

DA_HEADS = 8
DA_HEAD_DIM = 64
DA_V_DIM = 2 * DA_HEAD_DIM
DA_QK_WIDTH = DA_HEADS * 2 * DA_HEAD_DIM
DA_V_WIDTH = DA_HEADS * DA_V_DIM
DA_Q_BLOCK = 128
SSD_D_INNER = 2 * D_MODEL
SSD_HEAD_DIM = 64
SSD_HEADS = SSD_D_INNER // SSD_HEAD_DIM
SSD_GROUPS = 4
SSD_HEADS_PER_GROUP = SSD_HEADS // SSD_GROUPS
SSD_D_STATE = 128
SSD_BC_WIDTH = SSD_GROUPS * SSD_D_STATE
SSD_XBC_WIDTH = SSD_D_INNER + 2 * SSD_BC_WIDTH
SSD_CONV = 4
SSD_CHUNK = 256
DT_MIN = 0.001
DT_MAX = 0.1
N_BRANCHES = 2
IN_SPLITS = (DA_QK_WIDTH, DA_QK_WIDTH, DA_V_WIDTH, SSD_D_INNER, SSD_XBC_WIDTH, SSD_HEADS, N_BRANCHES * D_MODEL)
IN_WIDTH = sum(IN_SPLITS)
PEER_N_KEYS = 128
PEER_N_EXPERTS = PEER_N_KEYS * PEER_N_KEYS
PEER_HEADS = 8
PEER_TOPK = 16
PEER_QUERY_DIM = 256
PEER_HALF_DIM = PEER_QUERY_DIM // 2
PEER_TOKEN_BLOCK = 512
ALPHA = (2 * DEPTH) ** 0.25
BETA = (8 * DEPTH) ** -0.25
EPS = 1e-5


def layer_norm(x, g, b):
    xf = x.astype(jnp.float32)
    mu = jnp.mean(xf, axis=-1, keepdims=True)
    var = jnp.mean(jnp.square(xf - mu), axis=-1, keepdims=True)
    return ((xf - mu) * lax.rsqrt(var + EPS) * g + b).astype(x.dtype)

def rms_norm(x, w):
    xf = x.astype(jnp.float32)
    return (xf * lax.rsqrt(jnp.mean(jnp.square(xf), axis=-1, keepdims=True) + EPS) * w).astype(x.dtype)

def alibi_slopes(n):
    return jnp.asarray([2.0 ** (-8.0 * (i + 1) / n) for i in range(n)], jnp.float32)

def diff_attention(q, k, v, lam, lambda_init, subln_w):
    bsz, s = q.shape[:2]
    scale = DA_HEAD_DIM ** -0.5
    slopes = alibi_slopes(DA_HEADS)
    outs = []
    for i in range(s // DA_Q_BLOCK):
        q0 = i * DA_Q_BLOCK
        kend = q0 + DA_Q_BLOCK
        scores = jnp.einsum('bqhjd,bkhjd->bhjqk', q[:, q0:kend], k[:, :kend]).astype(jnp.float32) * scale
        dist = (jnp.arange(q0, kend)[:, None] - jnp.arange(kend)[None, :]).astype(jnp.float32)
        bias = jnp.where(dist[None] >= 0, -slopes[:, None, None] * dist[None], -jnp.inf)
        p = jax.nn.softmax(scores + bias[None, :, None], axis=-1)
        a = p[:, :, 0] - lam * p[:, :, 1]
        outs.append(jnp.einsum('bhqk,bkhe->bqhe', a.astype(v.dtype), v[:, :kend]))
    o = jnp.concatenate(outs, axis=1)
    o = rms_norm(o, subln_w) * (1.0 - lambda_init)
    return o.reshape(bsz, s, DA_V_WIDTH)

def causal_depthwise_conv(u, w, b):
    out = lax.conv_general_dilated(u, w[:, None, :].astype(u.dtype), window_strides=(1,),
                                   padding=[(SSD_CONV - 1, 0)], dimension_numbers=('NWC', 'WIO', 'NWC'),
                                   feature_group_count=u.shape[-1])
    return out + b

def ssd_chunked_scan(xh, dt, a, b_in, c_in):
    bsz, s = xh.shape[:2]
    pad = (-s) % SSD_CHUNK
    def padt(t):
        return jnp.pad(t, [(0, 0), (0, pad)] + [(0, 0)] * (t.ndim - 2))
    xh, dt, b_in, c_in = padt(xh), padt(dt), padt(b_in), padt(c_in)
    n_chunks = (s + pad) // SSD_CHUNK
    r = SSD_HEADS_PER_GROUP
    def chunks(t, tail):
        return t.reshape((bsz, n_chunks, SSD_CHUNK) + tail).swapaxes(0, 1)
    xs = (chunks(xh, (SSD_GROUPS, r, SSD_HEAD_DIM)), chunks(dt, (SSD_GROUPS, r)),
          chunks(b_in, (SSD_GROUPS, SSD_D_STATE)), chunks(c_in, (SSD_GROUPS, SSD_D_STATE)))
    a_gr = a.reshape(SSD_GROUPS, r)
    causal = jnp.tril(jnp.ones((SSD_CHUNK, SSD_CHUNK), dtype=bool))[None, :, :, None, None]

    def step(state, inp):
        xc, dtc, bc, cc = inp
        cum = jnp.cumsum(dtc * a_gr, axis=1)
        seg = cum[:, :, None] - cum[:, None, :]
        decay_ts = jnp.exp(jnp.where(causal, seg, -jnp.inf))
        cb = jnp.einsum('btgn,bsgn->btsg', cc, bc)
        w = cb[..., None] * decay_ts * dtc[:, None]
        y = jnp.einsum('btsgr,bsgrp->btgrp', w, xc)
        y = y + jnp.einsum('btgn,bgrpn->btgrp', cc, state) * jnp.exp(cum)[..., None]
        decay_end = jnp.exp(cum[:, -1:] - cum) * dtc
        state = state * jnp.exp(cum[:, -1])[..., None, None] + jnp.einsum('bsgn,bsgrp->bgrpn', bc, decay_end[..., None] * xc)
        return state, y

    state0 = jnp.zeros((bsz, SSD_GROUPS, r, SSD_HEAD_DIM, SSD_D_STATE), jnp.float32)
    _, ys = lax.scan(step, state0, xs)
    ys = ys.swapaxes(0, 1).reshape(bsz, n_chunks * SSD_CHUNK, SSD_HEADS, SSD_HEAD_DIM)
    return ys[:, :s]

def mamba2_branch(z, xbc, dt_raw, conv_w, conv_b, dt_bias, a_log, d_skip, norm_w):
    bsz, s = z.shape[:2]
    f32 = jnp.float32
    xbc = jax.nn.silu(causal_depthwise_conv(xbc, conv_w, conv_b))
    xs, b_in, c_in = jnp.split(xbc, [SSD_D_INNER, SSD_D_INNER + SSD_BC_WIDTH], axis=-1)
    xh = xs.reshape(bsz, s, SSD_HEADS, SSD_HEAD_DIM).astype(f32)
    dt = jax.nn.softplus(dt_raw.astype(f32) + dt_bias)
    a = -jnp.exp(a_log.astype(f32))
    y = ssd_chunked_scan(xh, dt, a,
                         b_in.reshape(bsz, s, SSD_GROUPS, SSD_D_STATE).astype(f32),
                         c_in.reshape(bsz, s, SSD_GROUPS, SSD_D_STATE).astype(f32))
    y = y + d_skip.astype(f32)[:, None] * xh
    y = y.reshape(bsz, s, SSD_D_INNER) * jax.nn.silu(z.astype(f32))
    y = rms_norm(y.reshape(bsz, s, SSD_GROUPS, SSD_D_INNER // SSD_GROUPS),
                 norm_w.reshape(SSD_GROUPS, -1)).reshape(bsz, s, SSD_D_INNER)
    return y.astype(z.dtype)

def peer_ffn(h, w_query, sub_keys, expert_u, expert_v):
    bsz, s, d = h.shape
    n_tok = bsz * s
    pad = (-n_tok) % PEER_TOKEN_BLOCK
    blocks = jnp.pad(h.reshape(n_tok, d), ((0, pad), (0, 0))).reshape(-1, PEER_TOKEN_BLOCK, d)

    def one_block(tb):
        q = (tb @ w_query).reshape(-1, PEER_HEADS, 2, PEER_HALF_DIM)
        sc = jnp.einsum('thjd,jkd->thjk', q, sub_keys).astype(jnp.float32)
        val, idx = lax.top_k(sc, PEER_TOPK)
        cand_s = val[:, :, 0, :, None] + val[:, :, 1, None, :]
        cand_i = idx[:, :, 0, :, None] * PEER_N_KEYS + idx[:, :, 1, None, :]
        cand_s = cand_s.reshape(cand_s.shape[0], PEER_HEADS, PEER_TOPK * PEER_TOPK)
        cand_i = cand_i.reshape(cand_i.shape[0], PEER_HEADS, PEER_TOPK * PEER_TOPK)
        top_s, pos = lax.top_k(cand_s, PEER_TOPK)
        eidx = jnp.take_along_axis(cand_i, pos, axis=-1)
        g = jax.nn.softmax(top_s, axis=-1)
        act = jax.nn.gelu(jnp.einsum('thkd,td->thk', expert_u[eidx], tb), approximate=False)
        wts = (g * act.astype(jnp.float32)).astype(tb.dtype)
        return jnp.einsum('thk,thkd->td', wts, expert_v[eidx])

    out = lax.map(one_block, blocks)
    return out.reshape(-1, d)[:n_tok].reshape(bsz, s, d)

def first_inputs(seed: int = 0) -> dict:
    key = jax.random.key(seed)
    ks = jax.random.split(key, 28)
    f32 = jnp.float32
    L = DEPTH
    def nrm(k, shape, std):
        return jax.random.normal(k, shape, f32) * std
    dt0 = jnp.exp(jax.random.uniform(ks[7], (L, SSD_HEADS), f32) * (math.log(DT_MAX) - math.log(DT_MIN)) + math.log(DT_MIN))
    return {
        'x': nrm(ks[0], (BATCH, SEQ, D_MODEL), 1.0),
        'c': nrm(ks[1], (BATCH, D_MODEL), 1.0),
        'w_ada': nrm(ks[2], (L, D_MODEL, 6 * D_MODEL), 0.5 * D_MODEL ** -0.5),
        'b_ada': nrm(ks[3], (L, 6 * D_MODEL), 0.02),
        'w_in': nrm(ks[4], (L, D_MODEL, IN_WIDTH), D_MODEL ** -0.5),
        'conv_w': nrm(ks[5], (L, SSD_CONV, SSD_XBC_WIDTH), SSD_CONV ** -0.5),
        'conv_b': nrm(ks[6], (L, SSD_XBC_WIDTH), 0.02),
        'dt_bias': dt0 + jnp.log(-jnp.expm1(-dt0)),
        'a_log': jnp.log(jax.random.uniform(ks[8], (L, SSD_HEADS), f32, 1.0, 16.0)),
        'd_skip': 1.0 + nrm(ks[9], (L, SSD_HEADS), 0.1),
        'ssd_norm_w': 1.0 + nrm(ks[10], (L, SSD_D_INNER), 0.1),
        'lambda_q1': nrm(ks[11], (L, DA_HEAD_DIM), 0.1),
        'lambda_k1': nrm(ks[12], (L, DA_HEAD_DIM), 0.1),
        'lambda_q2': nrm(ks[13], (L, DA_HEAD_DIM), 0.1),
        'lambda_k2': nrm(ks[14], (L, DA_HEAD_DIM), 0.1),
        'da_subln_w': 1.0 + nrm(ks[15], (L, DA_V_DIM), 0.1),
        'w_attn_branch': nrm(ks[16], (L, DA_V_WIDTH, D_MODEL), DA_V_WIDTH ** -0.5),
        'w_ssd_branch': nrm(ks[17], (L, SSD_D_INNER, D_MODEL), SSD_D_INNER ** -0.5),
        'w_out': nrm(ks[18], (L, D_MODEL, D_MODEL), BETA * D_MODEL ** -0.5),
        'ln1_g': 1.0 + nrm(ks[19], (L, D_MODEL), 0.1),
        'ln1_b': nrm(ks[20], (L, D_MODEL), 0.02),
        'peer_w_query': nrm(ks[21], (L, D_MODEL, PEER_HEADS * PEER_QUERY_DIM), D_MODEL ** -0.5),
        'peer_sub_keys': nrm(ks[22], (L, 2, PEER_N_KEYS, PEER_HALF_DIM), PEER_HALF_DIM ** -0.5),
        'peer_u': nrm(ks[23], (L, PEER_N_EXPERTS, D_MODEL), D_MODEL ** -0.5),
        'peer_v': nrm(ks[24], (L, PEER_N_EXPERTS, D_MODEL), BETA * PEER_HEADS ** -0.5),
        'ln2_g': 1.0 + nrm(ks[25], (L, D_MODEL), 0.1),
        'ln2_b': nrm(ks[26], (L, D_MODEL), 0.02),
    }

def first_block(x, c, w_ada, b_ada, w_in, conv_w, conv_b, dt_bias, a_log, d_skip, ssd_norm_w,
              lambda_q1, lambda_k1, lambda_q2, lambda_k2, da_subln_w, w_attn_branch, w_ssd_branch,
              w_out, ln1_g, ln1_b, peer_w_query, peer_sub_keys, peer_u, peer_v, ln2_g, ln2_b):
    bsz, s, _ = x.shape
    split_at = np.cumsum(IN_SPLITS)[:-1].tolist()
    f32 = jnp.float32
    for l in range(DEPTH):
        mod = jax.nn.silu(c) @ w_ada[l] + b_ada[l]
        shift1, scale1, gate1, shift2, scale2, gate2 = jnp.split(mod[:, None, :], 6, axis=-1)
        h = x * (1.0 + scale1) + shift1
        q, k, v, z, xbc, dt_raw, g_logits = jnp.split(h @ w_in[l], split_at, axis=-1)
        lambda_init = 0.8 - 0.6 * math.exp(-0.3 * l)
        lam = (jnp.exp(jnp.sum(lambda_q1[l].astype(f32) * lambda_k1[l].astype(f32)))
               - jnp.exp(jnp.sum(lambda_q2[l].astype(f32) * lambda_k2[l].astype(f32))) + lambda_init)
        y_attn = diff_attention(q.reshape(bsz, s, DA_HEADS, 2, DA_HEAD_DIM),
                                k.reshape(bsz, s, DA_HEADS, 2, DA_HEAD_DIM),
                                v.reshape(bsz, s, DA_HEADS, DA_V_DIM),
                                lam, lambda_init, da_subln_w[l]) @ w_attn_branch[l]
        y_ssd = mamba2_branch(z, xbc, dt_raw, conv_w[l], conv_b[l], dt_bias[l], a_log[l],
                              d_skip[l], ssd_norm_w[l]) @ w_ssd_branch[l]
        g_attn, g_ssd = jnp.split(jax.nn.sigmoid(g_logits), N_BRANCHES, axis=-1)
        mixed = (g_attn * y_attn + g_ssd * y_ssd) @ w_out[l]
        x = layer_norm(ALPHA * x + gate1 * mixed, ln1_g[l], ln1_b[l])
        h2 = x * (1.0 + scale2) + shift2
        y_ffn = peer_ffn(h2, peer_w_query[l], peer_sub_keys[l], peer_u[l], peer_v[l])
        x = layer_norm(ALPHA * x + gate2 * y_ffn, ln2_g[l], ln2_b[l])
    return x


DEPTH_2 = 2

CHUNK = 64
N_MIXERS = 2
N_RWKV = (DEPTH_2 + 1) // 2
N_MLSTM = DEPTH_2 // 2
EPS_2 = 1e-6
NEG = -1e30

RW_HEAD = 64
RW_HEADS = D_MODEL // RW_HEAD
LORA_W = 64
LORA_A = 64
LORA_G = 160
RW_SEGS = (D_MODEL, LORA_W, D_MODEL, D_MODEL, LORA_A, LORA_G)
RW_IN = sum(RW_SEGS)
GN_EPS = 64e-5

ML_HEADS = 8
ML_QK = D_MODEL // 2 // ML_HEADS
ML_V = D_MODEL // ML_HEADS
ML_QKW = 2 * ML_HEADS * ML_QK
ML_VW = ML_HEADS * ML_V
ML_IN = ML_QKW + 2 * ML_VW + 2 * ML_HEADS
CONV_W = 4
GATE_CAP = 15.0

D_FF = -(-(8 * D_MODEL) // (3 * 256)) * 256


def _rms(x):
    xf = x.astype(jnp.float32)
    return (xf * lax.rsqrt(jnp.mean(xf * xf, -1, keepdims=True) + EPS_2)).astype(x.dtype)

def _softcap(t):
    return GATE_CAP * jnp.tanh(t / GATE_CAP)

def _token_shift(x):
    return jnp.pad(x[:, :-1], ((0, 0), (1, 0), (0, 0)))

def _rwkv7_step(state, inp):
    r_t, w_t, k_t, v_t, a_t, b_t = inp
    sa = jnp.einsum('bhvk,bhk->bhv', state, a_t)
    state = state * w_t[:, :, None, :] + sa[..., None] * b_t[:, :, None, :] + v_t[..., None] * k_t[:, :, None, :]
    y = jnp.einsum('bhvk,bhk->bhv', state, r_t)
    return state, y

def _rwkv7_mix(x, mix, w_in, w0, w2, a0, a2, g2, k_k, k_a, r_k, gn_w, gn_b, w_out):
    B, S, D = x.shape
    xx = _token_shift(x) - x
    xs = x[None] + xx[None] * mix[:, None, None, :]
    outs = []
    off = 0
    for i, n in enumerate(RW_SEGS):
        outs.append(xs[i] @ w_in[:, off:off + n])
        off += n
    r, wl, k, v, al, gl = outs
    w_log = -jax.nn.softplus(-(w0 + jnp.tanh(wl) @ w2)) - 0.5
    decay = jnp.exp(-jnp.exp(w_log.astype(jnp.float32)))
    a = jax.nn.sigmoid(a0 + al @ a2)
    g = jax.nn.sigmoid(gl) @ g2
    hs = lambda t: t.reshape(B, S, RW_HEADS, RW_HEAD).astype(jnp.float32)
    kk = hs(k * k_k)
    kk = kk / jnp.maximum(jnp.linalg.norm(kk, axis=-1, keepdims=True), 1e-12)
    k = k * (1.0 + (a - 1.0) * k_a)
    rh, kh, vh, ah, wh = hs(r), hs(k), hs(v), hs(a), hs(decay)
    tm = lambda t: jnp.moveaxis(t, 1, 0)
    state0 = jnp.zeros((B, RW_HEADS, RW_HEAD, RW_HEAD), jnp.float32)
    _, y = lax.scan(_rwkv7_step, state0, (tm(rh), tm(wh), tm(kh), tm(vh), tm(-kk), tm(kk * ah)))
    y = jnp.moveaxis(y, 0, 1)
    mu = jnp.mean(y, -1, keepdims=True)
    var = jnp.mean(jnp.square(y - mu), -1, keepdims=True)
    y = ((y - mu) * lax.rsqrt(var + GN_EPS)).reshape(B, S, D) * gn_w + gn_b
    bonus = (jnp.sum(rh * kh * r_k, -1, keepdims=True) * vh).reshape(B, S, D)
    return ((y + bonus).astype(x.dtype) * g) @ w_out

def _causal_dwconv(x, w, b):
    y = lax.conv_general_dilated(x, w[:, None, :], window_strides=(1,), padding=[(CONV_W - 1, 0)],
                                 dimension_numbers=('NWC', 'WIO', 'NWC'), feature_group_count=x.shape[-1])
    return y + b

def _mlstm_chunk_step(carry, inp):
    C, n, m = carry
    g_c, m_l, C_l, n_l = inp
    m_new = jnp.maximum(g_c + m, m_l)
    sa = jnp.exp(g_c + m - m_new)
    sb = jnp.exp(m_l - m_new)
    C_new = sa[..., None, None] * C + sb[..., None, None] * C_l
    n_new = sa[..., None] * n + sb[..., None] * n_l
    return (C_new, n_new, m_new), (C, n, m)

def _mlstm_mix(x, w_in, conv_w, conv_b, b_i, b_f, hn_w, w_out):
    B, S, D = x.shape
    NC = S // CHUNK
    p = x @ w_in
    qk = jax.nn.silu(_causal_dwconv(p[..., :ML_QKW], conv_w, conv_b))
    v = p[..., ML_QKW:ML_QKW + ML_VW]
    o = p[..., ML_QKW + ML_VW:ML_QKW + 2 * ML_VW]
    gi = p[..., ML_QKW + 2 * ML_VW:ML_QKW + 2 * ML_VW + ML_HEADS]
    gf = p[..., ML_QKW + 2 * ML_VW + ML_HEADS:]
    chunks = lambda t, dh: t.reshape(B, NC, CHUNK, ML_HEADS, dh).transpose(0, 3, 1, 2, 4).astype(jnp.float32)
    q = chunks(qk[..., :ML_QKW // 2], ML_QK) * (ML_QK ** -0.5)
    k = chunks(qk[..., ML_QKW // 2:], ML_QK)
    v = chunks(v, ML_V)
    gate_chunks = lambda t: t.reshape(B, NC, CHUNK, ML_HEADS).transpose(0, 3, 1, 2)
    log_i = gate_chunks(_softcap(gi.astype(jnp.float32) + b_i))
    log_f = gate_chunks(jax.nn.log_sigmoid(_softcap(gf.astype(jnp.float32) + b_f)))
    bcum = jnp.cumsum(log_f, -1)
    causal = jnp.tril(jnp.ones((CHUNK, CHUNK), dtype=bool))
    d_log = jnp.where(causal, bcum[..., :, None] - bcum[..., None, :] + log_i[..., None, :], NEG)
    m_intra = jnp.max(d_log, -1)
    g_tot = bcum[..., -1]
    loc = g_tot[..., None] - bcum + log_i
    m_loc = jnp.max(loc, -1)
    wl = jnp.exp(loc - m_loc[..., None])
    C_loc = jnp.einsum('bhcs,bhcsd,bhcse->bhcde', wl, k, v)
    n_loc = jnp.einsum('bhcs,bhcsd->bhcd', wl, k)
    init = (jnp.zeros((B, ML_HEADS, ML_QK, ML_V), jnp.float32),
            jnp.zeros((B, ML_HEADS, ML_QK), jnp.float32),
            jnp.zeros((B, ML_HEADS), jnp.float32))
    cm = lambda t: jnp.moveaxis(t, 2, 0)
    _, (C_prev, n_prev, m_prev) = lax.scan(_mlstm_chunk_step, init, (cm(g_tot), cm(m_loc), cm(C_loc), cm(n_loc)))
    C_prev, n_prev, m_prev = jnp.moveaxis(C_prev, 0, 2), jnp.moveaxis(n_prev, 0, 2), jnp.moveaxis(m_prev, 0, 2)
    inter = bcum + m_prev[..., None]
    m_t = jnp.maximum(inter, m_intra)
    w_inter = jnp.exp(inter - m_t)
    w_intra = jnp.exp(d_log - m_t[..., None]) * jnp.einsum('bhctd,bhcsd->bhcts', q, k)
    num = w_inter[..., None] * jnp.einsum('bhctd,bhcde->bhcte', q, C_prev) + jnp.einsum('bhcts,bhcse->bhcte', w_intra, v)
    den = w_inter * jnp.einsum('bhctd,bhcd->bhct', q, n_prev) + jnp.sum(w_intra, -1)
    den = jnp.maximum(jnp.abs(den), jnp.exp(-m_t))
    h = num / den[..., None]
    h = h * lax.rsqrt(jnp.mean(h * h, -1, keepdims=True) + EPS_2) * hn_w[:, None, None, :]
    h = h.transpose(0, 2, 3, 1, 4).reshape(B, S, ML_VW).astype(x.dtype)
    return (h * jax.nn.sigmoid(o)) @ w_out

def _swiglu(x, w_gu, w_down):
    gu = x @ w_gu
    return (jax.nn.silu(gu[..., :D_FF]) * gu[..., D_FF:]) @ w_down

def second_inputs(seed: int = 0) -> dict:
    key = jax.random.key(seed)
    ks = jax.random.split(key, 32)
    nrm = lambda i, shape, s: jax.random.normal(ks[i], shape, jnp.float32) * s
    D = D_MODEL
    lin = jnp.arange(D, dtype=jnp.float32) / (D - 1)
    return {
        "x": nrm(0, (BATCH, SEQ, D), 1.0),
        "c": nrm(1, (BATCH, D), 1.0),
        "ada_w": nrm(2, (DEPTH_2, D, 6 * D), 0.3 * D ** -0.5),
        "ada_b": nrm(3, (DEPTH_2, 6 * D), 0.02),
        "rw_mix": jax.random.uniform(ks[4], (N_RWKV, 6, D), jnp.float32),
        "rw_w_in": nrm(5, (N_RWKV, D, RW_IN), D ** -0.5),
        "rw_w0": jnp.broadcast_to(-6.0 + 5.0 * lin ** 1.5, (N_RWKV, D)) + nrm(6, (N_RWKV, D), 0.1),
        "rw_w2": nrm(7, (N_RWKV, LORA_W, D), 0.3 * LORA_W ** -0.5),
        "rw_a0": nrm(8, (N_RWKV, D), 0.1),
        "rw_a2": nrm(9, (N_RWKV, LORA_A, D), LORA_A ** -0.5),
        "rw_g2": nrm(10, (N_RWKV, LORA_G, D), LORA_G ** -0.5),
        "rw_k_k": 0.85 + nrm(11, (N_RWKV, D), 0.05),
        "rw_k_a": 1.0 + nrm(12, (N_RWKV, D), 0.05),
        "rw_r_k": nrm(13, (N_RWKV, RW_HEADS, RW_HEAD), 0.1),
        "rw_gn_w": 1.0 + nrm(14, (N_RWKV, D), 0.05),
        "rw_gn_b": nrm(15, (N_RWKV, D), 0.02),
        "rw_w_out": nrm(16, (N_RWKV, D, D), D ** -0.5),
        "ml_w_in": nrm(17, (N_MLSTM, D, ML_IN), D ** -0.5),
        "ml_conv_w": nrm(18, (N_MLSTM, CONV_W, ML_QKW), CONV_W ** -0.5),
        "ml_conv_b": nrm(19, (N_MLSTM, ML_QKW), 0.02),
        "ml_b_i": nrm(20, (N_MLSTM, ML_HEADS), 0.1),
        "ml_b_f": jnp.broadcast_to(jnp.linspace(3.0, 6.0, ML_HEADS, dtype=jnp.float32), (N_MLSTM, ML_HEADS)) + nrm(21, (N_MLSTM, ML_HEADS), 0.1),
        "ml_hn_w": 1.0 + nrm(22, (N_MLSTM, ML_HEADS, ML_V), 0.05),
        "ml_w_out": nrm(23, (N_MLSTM, D, D), D ** -0.5),
        "ffn_w_gu": nrm(24, (DEPTH_2, D, 2 * D_FF), D ** -0.5),
        "ffn_w_down": nrm(25, (DEPTH_2, D_FF, D), D_FF ** -0.5),
        "final_w": 1.0 + nrm(26, (D,), 0.05),
    }

def second_block(x, c, ada_w, ada_b, rw_mix, rw_w_in, rw_w0, rw_w2, rw_a0, rw_a2, rw_g2, rw_k_k, rw_k_a,
              rw_r_k, rw_gn_w, rw_gn_b, rw_w_out, ml_w_in, ml_conv_w, ml_conv_b, ml_b_i, ml_b_f, ml_hn_w,
              ml_w_out, ffn_w_gu, ffn_w_down, final_w):
    c_act = jax.nn.silu(c)
    for i in range(DEPTH_2):
        mod = c_act @ ada_w[i] + ada_b[i]
        sh1, sc1, g1, sh2, sc2, g2 = [t[:, None, :] for t in jnp.split(mod, 6, axis=-1)]
        h = _rms(x) * (1.0 + sc1) + sh1
        j = i // N_MIXERS
        if i % N_MIXERS == 0:
            y = _rwkv7_mix(h, rw_mix[j], rw_w_in[j], rw_w0[j], rw_w2[j], rw_a0[j], rw_a2[j], rw_g2[j],
                           rw_k_k[j], rw_k_a[j], rw_r_k[j], rw_gn_w[j], rw_gn_b[j], rw_w_out[j])
        else:
            y = _mlstm_mix(h, ml_w_in[j], ml_conv_w[j], ml_conv_b[j], ml_b_i[j], ml_b_f[j], ml_hn_w[j], ml_w_out[j])
        x = x + g1 * y
        h = _rms(x) * (1.0 + sc2) + sh2
        x = x + g2 * _swiglu(h, ffn_w_gu[i], ffn_w_down[i])
    return _rms(x) * final_w


def setup_inputs(seed=0):
    out = dict(first_inputs(seed))
    for name, value in second_inputs(seed + 1).items():
        if name != "x":
            out[name + "_2"] = value
    return out


def reference(
    x, c, w_ada, b_ada, w_in, conv_w, conv_b, dt_bias, a_log, d_skip, ssd_norm_w, lambda_q1,
    lambda_k1, lambda_q2, lambda_k2, da_subln_w, w_attn_branch, w_ssd_branch, w_out, ln1_g,
    ln1_b, peer_w_query, peer_sub_keys, peer_u, peer_v, ln2_g, ln2_b, c_2, ada_w_2, ada_b_2,
    rw_mix_2, rw_w_in_2, rw_w0_2, rw_w2_2, rw_a0_2, rw_a2_2, rw_g2_2, rw_k_k_2, rw_k_a_2,
    rw_r_k_2, rw_gn_w_2, rw_gn_b_2, rw_w_out_2, ml_w_in_2, ml_conv_w_2, ml_conv_b_2, ml_b_i_2,
    ml_b_f_2, ml_hn_w_2, ml_w_out_2, ffn_w_gu_2, ffn_w_down_2, final_w_2,
):
    x = first_block(
        x, c, w_ada, b_ada, w_in, conv_w, conv_b, dt_bias, a_log, d_skip, ssd_norm_w, lambda_q1,
        lambda_k1, lambda_q2, lambda_k2, da_subln_w, w_attn_branch, w_ssd_branch, w_out, ln1_g,
        ln1_b, peer_w_query, peer_sub_keys, peer_u, peer_v, ln2_g, ln2_b,
    )
    return second_block(
        x, c_2, ada_w_2, ada_b_2, rw_mix_2, rw_w_in_2, rw_w0_2, rw_w2_2, rw_a0_2, rw_a2_2,
        rw_g2_2, rw_k_k_2, rw_k_a_2, rw_r_k_2, rw_gn_w_2, rw_gn_b_2, rw_w_out_2, ml_w_in_2,
        ml_conv_w_2, ml_conv_b_2, ml_b_i_2, ml_b_f_2, ml_hn_w_2, ml_w_out_2, ffn_w_gu_2,
        ffn_w_down_2, final_w_2,
    )


_drawn_inputs = setup_inputs


def setup_inputs(seed=0):
    import zlib

    import numpy as np

    out = dict(_drawn_inputs(seed))
    spreads = {}
    factors = {'b_ada': 5.397,
     'conv_b': 8.0,
     'd_skip': 8.0,
     'ssd_norm_w': 6.539,
     'lambda_q1': 5.484,
     'lambda_k1': 8.0,
     'lambda_q2': 8.0,
     'lambda_k2': 8.0,
     'da_subln_w': 7.525,
     'rw_w2_2': 8.0,
     'rw_a0_2': 8.0,
     'rw_k_k_2': 8.0,
     'rw_k_a_2': 8.0,
     'rw_gn_w_2': 8.0,
     'rw_gn_b_2': 23.952,
     'ml_conv_b_2': 8.0,
     'ml_b_i_2': 64.0,
     'ml_hn_w_2': 8.0}
    for name, (base, spread) in spreads.items():
        noise = np.random.default_rng([zlib.crc32(name.encode()), seed]).standard_normal(out[name].shape)
        drawn = base * np.exp(spread * noise) if base else spread * noise
        out[name] = jnp.asarray(drawn.astype(out[name].dtype))
    for name, factor in factors.items():
        out[name] = (out[name] * factor).astype(out[name].dtype)
    return out
```

```python
from contextlib import ExitStack

import numpy as np

import concourse.bass as bass
from concourse import mybir

ALU = mybir.AluOpType
ACT = mybir.ActivationFunctionType
AX_X = mybir.AxisListType.X
F32 = mybir.dt.float32
I32 = mybir.dt.int32
U32 = mybir.dt.uint32

P = 128
S = 512
D = 1024
KT = D // P
TB = S // P
ALPHA = 2.0 ** 0.25
EPS_LN = 1e-5
EPS_RMS = 1e-6
EPS_GN = 64e-5

HEADS_DA = 8
T_Q, T_K, T_V, T_Z, T_XS, T_B, T_C, T_GA, T_GS = 0, 8, 16, 24, 40, 56, 60, 64, 72
SSD_TILES = 16
SSD_GROUPS = 4
SSD_HEADS = 32

VEC_PARTS = [
    ("c", 8), ("c2", 8), ("b_ada", 48), ("ada_b2", 96),
    ("conv_w0", 24), ("conv_w1", 24), ("conv_w2", 24), ("conv_w3", 24), ("conv_b", 24),
    ("d_skip", 16), ("ssd_norm", 16), ("subln", 1), ("lam", 4), ("head_ssd", 2), ("head_ml", 2),
    ("ln1_g", 8), ("ln1_b", 8), ("ln2_g", 8), ("ln2_b", 8),
    ("mix", 48), ("w0", 8), ("a0", 8), ("k_k", 8), ("k_a", 8), ("r_k", 8), ("gn_w", 8), ("gn_b", 8),
    ("ml_w0", 8), ("ml_w1", 8), ("ml_w2", 8), ("ml_w3", 8), ("ml_cb", 8), ("hn_w", 8), ("final", 8),
]
VEC_AT = {}
_at = 0
for _name, _n in VEC_PARTS:
    VEC_AT[_name] = _at
    _at += _n
VEC_COLS = _at


def ds(start, n):
    return bass.ds(start, n)


class Chain:

    def __init__(self, eng, sem):
        self.eng, self.sem, self.n = eng, sem, 0

    def restart(self):
        self.eng.sem_clear(self.sem)
        self.n = 0

    def __call__(self, ins):
        ins.then_inc(self.sem, 1)
        self.n += 1
        self.eng.wait_ge(self.sem, self.n)


class Phase:

    def __init__(self, nc, name):
        self.nc, self.name, self.sems, self.ctx = nc, name, [], ExitStack()

    def __enter__(self):
        self.ctx.__enter__()
        return self

    def sb(self, name, shape, dt=F32):
        return self.ctx.enter_context(self.nc.sbuf_tensor(f"{self.name}_{name}", shape, dt))

    def ps(self, name, shape, dt=F32):
        return self.ctx.enter_context(self.nc.psum_tensor(f"{self.name}_{name}", shape, dt))

    def sem(self, name):
        s = self.ctx.enter_context(self.nc.semaphore(f"{self.name}_{name}"))
        self.sems.append(s)
        return s

    def block(self):
        return self.nc.Block()

    def __exit__(self, *a):
        if a[0] is None and self.sems:
            nums = [s.num for s in self.sems]
            self.nc.all_engine_barrier(sems_to_clear=range(min(nums), max(nums) + 1))
        return self.ctx.__exit__(*a)


def product(nc, out, w, x, n):
    for k in range(n):
        last = nc.tensor.matmul(out, w[:, k], x[:, k], start=(k == 0), stop=(k == n - 1))
    return last


def w_tile(dram, t, n=1):
    return dram[ds(t, n)].rearrange("a p k n -> (a p) k n")


def tile_at(buf, t):
    return buf[:, ds(t, 1)].rearrange("p a n -> p (a n)")



def setup_phase(nc, io, C):
    with Phase(nc, "setup") as ph:
        loaded, made, chain_s, v_s = ph.sem("loaded"), ph.sem("made"), ph.sem("chain"), ph.sem("vchain")
        act_s = ph.sem("act")
        row_i, col_i = ph.sb("row_i", [P, P], I32), ph.sb("col_i", [P, P], I32)
        rs, cs = ph.sb("rs", [P, P], I32), ph.sb("cs", [P, P], I32)
        rf, cf = ph.sb("rf", [P, P]), ph.sb("cf", [P, P])
        dist_i = ph.sb("dist_i", [P, S], I32)
        same = ph.sb("same", [P, 7, P])
        strict = ph.sb("strict", [P, P])
        lamp = ph.sb("lamp", [P, 2])
        lame = ph.sb("lame", [P, 2])
        ps = ph.ps("ps", [P, 2])
        lsum = ph.sem("lsum")
        with ph.block() as block:
            @block.sync
            def _(sp):
                sp.dma_start(C.X[:], io["x"]).then_inc(loaded, 16)
                sp.dma_start(C.vec[:], io["vec"]).then_inc(loaded, 16)

            @block.gpsimd
            def _(pool):
                link = Chain(pool, chain_s)
                link(nc.gpsimd.memset(C.ones[:], 1.0))
                link(nc.gpsimd.memset(C.ident[:], 0.0))
                link(nc.gpsimd.affine_select(out=C.ident[:], in_=C.ident[:], compare_op=ALU.not_equal, fill=1.0,
                                             base=0, pattern=[[-1, P]], channel_multiplier=1))
                link(nc.gpsimd.affine_select(out=C.keep[:], in_=C.ones[:], compare_op=ALU.is_ge, fill=0.0,
                                             base=0, pattern=[[1, P]], channel_multiplier=-1))
                link(nc.gpsimd.affine_select(out=strict[:], in_=C.ones[:], compare_op=ALU.is_gt, fill=0.0,
                                             base=0, pattern=[[1, P]], channel_multiplier=-1))
                for h in range(2):
                    r = slice(64 * h, 64 * h + 64)
                    link(nc.gpsimd.affine_select(out=C.keep64[r], in_=C.ones[r, 0:64], compare_op=ALU.is_ge, fill=0.0,
                                                 base=0, pattern=[[1, 64]], channel_multiplier=-1))
                link(nc.gpsimd.iota(dist_i[:], pattern=[[-1, S]], base=S - P, channel_multiplier=1))
                link(nc.gpsimd.tensor_copy(C.dist[:], dist_i[:]))
                link(nc.gpsimd.affine_select(out=C.dist[:], in_=C.dist[:], compare_op=ALU.is_ge, fill=1e30,
                                             base=S - P, pattern=[[-1, S]], channel_multiplier=1))
                link(nc.gpsimd.iota(row_i[:], pattern=[[0, P]], base=0, channel_multiplier=1))
                link(nc.gpsimd.iota(col_i[:], pattern=[[1, P]], base=0, channel_multiplier=0))
                link(nc.gpsimd.tensor_copy(C.iota[:], col_i[:]))
                for h in range(HEADS_DA):
                    link(nc.gpsimd.memset(C.nslope[:, h:h + 1], -8.0 * 2.0 ** (-(h + 1))))
                link(nc.gpsimd.memset(C.carry[:], 1.0))
                nc.gpsimd.memset(C.carry[:].rearrange("p (c t) -> p c t", t=64)[:, :, 0:1], 0.0).then_inc(made, 1)

            @block.vector
            def _(dve):
                link = Chain(dve, v_s)
                dve.wait_ge(made, 1)
                for n in range(8):
                    if n < 7:
                        for src, i, f in ((row_i, rs, rf), (col_i, cs, cf)):
                            link(nc.vector.tensor_scalar(i[:], src[:], n, None, ALU.arith_shift_right))
                            link(nc.vector.tensor_copy(f[:], i[:]))
                        link(nc.vector.tensor_tensor(same[:, n], rf[:], cf[:], ALU.is_equal))
                link(nc.vector.tensor_copy(C.ones_bd[:], same[:, 6]))
                for n in range(6):
                    link(nc.vector.tensor_tensor(C.level[:, n], same[:, n + 1], same[:, n], ALU.subtract))
                    link(nc.vector.tensor_tensor(C.level[:, n], C.level[:, n], strict[:], ALU.mult))
                link(nc.vector.tensor_copy(C.strict[:], strict[:]))
                dve.wait_ge(loaded, 32)
                lam = C.v("lam", 0, 4)
                link(nc.vector.tensor_tensor(lamp[:], lam[:, 0:4:2], lam[:, 1:4:2], ALU.mult))
                dve.sem_inc(lsum, 1)
                dve.wait_ge(act_s, 1)
                link(nc.vector.tensor_tensor(C.nlam[:], lame[:, 1:2], lame[:, 0:1], ALU.subtract))
                link(nc.vector.tensor_scalar(C.nlam[:], C.nlam[:], -0.2, None, ALU.add))
                link(nc.vector.tensor_scalar(C.subln[:], C.v("subln", 0), 0.8, None, ALU.mult))

            @block.tensor
            def _(pe):
                pe.wait_ge(made, 1)
                pe.wait_ge(lsum, 1)
                nc.tensor.matmul(ps[:], C.ones[:], lamp[:], start=True, stop=True).then_inc(lsum, 1)

            @block.scalar
            def _(act):
                act.wait_ge(lsum, 2)
                nc.scalar.activation(lame[:], ps[:], ACT.Exp).then_inc(act_s, 1)
                act.wait_ge(loaded, 32)
                nc.scalar.activation(C.csil[:, 0:16], C.v("c", 0, 16), ACT.Silu)


def ada_phase(nc, io, C):
    RING, CHUNK, STEPS, FIRST = 3, 512, 36, 12
    with Phase(nc, "ada") as ph:
        loaded = [ph.sem(f"loaded{r}") for r in range(RING)]
        weighted, summed, kept, chain_s = ph.sem("weighted"), ph.sem("summed"), ph.sem("kept"), ph.sem("chain")
        bias_s = ph.sem("biased")
        w = ph.sb("w", [P, RING, KT, CHUNK])
        part = ph.sb("part", [P, RING, CHUNK])
        acc = ph.ps("acc", [P, RING, 512])
        with ph.block() as block:
            @block.sync
            def _(sp):
                with sp.Fori(0, STEPS // RING) as i:
                    for r in range(RING):
                        sp.wait_ge(weighted, RING * i + r + 1)
                        sp.dma_start(w[:, r], w_tile(io["w_ada"], RING * i + r)).then_inc(loaded[r], 16)

            @block.vector
            def _(dve):
                link = Chain(dve, chain_s)

                def steps(i, col):
                    link.restart()
                    for r in range(RING):
                        dve.wait_ge(loaded[r], 16 * (i + 1))
                        dve.wait_ge(summed, RING * i + r + 1)
                        link(nc.vector.tensor_scalar(part[:, r], w[:, r, 0], C.csil[:, col:col + 1], None, ALU.mult))
                        for k in range(1, KT):
                            ins = nc.vector.scalar_tensor_tensor(out=part[:, r], in0=w[:, r, k],
                                                                 scalar=C.csil[:, col + k:col + k + 1],
                                                                 in1=part[:, r], op0=ALU.mult, op1=ALU.add)
                            if k < KT - 1:
                                link(ins)
                            else:
                                ins.then_inc(weighted, 1)
                dve.sem_inc(weighted, RING)
                with dve.Fori(0, FIRST // RING) as i:
                    steps(i, 0)
                with dve.Fori(FIRST // RING, STEPS // RING) as i:
                    steps(i, 8)

            @block.tensor
            def _(pe):
                pe.sem_inc(summed, RING)
                with pe.Fori(0, STEPS // RING) as i:
                    for r in range(RING):
                        pe.wait_ge(weighted, RING * i + r + 1 + RING)
                        pe.wait_ge(kept, RING * i + r + 1)
                        for n in range(CHUNK // P):
                            last = nc.tensor.matmul(acc[:, r, n:n + 1], part[:, r, n * P:(n + 1) * P],
                                                    C.ones[:, 0:1], start=True, stop=True)
                        last.then_inc(summed, 1)

            @block.scalar
            def _(act):
                act.sem_inc(kept, RING)
                with act.Fori(0, STEPS // RING) as i:
                    for r in range(RING):
                        act.wait_ge(summed, RING * i + r + 1 + RING)
                        nc.scalar.activation(C.mod[:, ds((i * RING + r) * 4, 4)], acc[:, r, 0:4], ACT.Copy
                                             ).then_inc(kept, 1)
        with ph.block() as block:
            @block.vector
            def _(dve):
                nc.vector.tensor_tensor(C.mod[:], C.mod[:], C.v("b_ada", 0, 144), ALU.add).then_inc(bias_s, 1)
                dve.wait_ge(bias_s, 1)
                for layer in range(3):
                    for part_n in (1, 4):
                        col = 48 * layer + 8 * part_n
                        nc.vector.tensor_scalar(C.mod[:, col:col + 8], C.mod[:, col:col + 8], 1.0, None, ALU.add)


def modulate_phase(nc, C, layer, part):
    with Phase(nc, f"modulate{layer}{part}") as ph:
        with ph.block() as block:
            @block.vector
            def _(dve):
                for k in range(KT):
                    nc.vector.tensor_scalar(C.H[:, k], C.X[:, k], C.m(layer, part + 1, k), C.m(layer, part, k),
                                            ALU.mult, ALU.add)


def norm_phase(nc, C, name, src, dst, groups, size, count, eps, weight=None, bias=None, center=False, mod=None,
               times=None):
    with Phase(nc, name) as ph:
        squared, summed, sqrt_in, rooted = (ph.sem(n) for n in ("squared", "summed", "sqrt_in", "rooted"))
        centered, averaged, chain_s = ph.sem("centered"), ph.sem("averaged"), ph.sem("chain")
        RING = 4
        sq = ph.sb("sq", [P, RING, S])
        mean = ph.sb("mean", [P, S])
        var = ph.sb("var", [P, 2, S])
        inv = ph.sb("inv", [P, 2, S])
        acc = ph.ps("acc", [P, 2, S])
        avg = ph.ps("avg", [P, S])
        tiles = groups * size
        with ph.block() as block:
            @block.tensor
            def _(pe):
                if center:
                    for t in range(tiles):
                        last = nc.tensor.matmul(avg[:], C.ones[:], src[:, t], start=(t == 0), stop=(t == tiles - 1))
                    last.then_inc(averaged, 1)
                for t in range(tiles):
                    g = t // size
                    pe.wait_ge(squared, t + 1)
                    if g >= 2:
                        pe.wait_ge(sqrt_in, g - 1)
                    nc.tensor.matmul(acc[:, g % 2], C.ones[:], sq[:, t % RING], start=(t % size == 0),
                                     stop=(t % size == size - 1)).then_inc(summed, 1)

            @block.scalar
            def _(act):
                def roots(g):
                    act.wait_ge(sqrt_in, g + 1)
                    nc.scalar.activation(var[:, g % 2], var[:, g % 2], ACT.Sqrt).then_inc(rooted, 1)
                for t in range(tiles):
                    if center:
                        act.wait_ge(centered, t + 1)
                    if t >= RING:
                        act.wait_ge(summed, t - RING + 1)
                    nc.scalar.activation(sq[:, t % RING], src[:, t], ACT.Square).then_inc(squared, 1)
                    if t % size == size - 1 and t // size >= 1:
                        roots(t // size - 1)
                roots(groups - 1)

            @block.vector
            def _(dve):
                link = Chain(dve, chain_s)
                if center:
                    dve.wait_ge(averaged, 1)
                    link(nc.vector.tensor_scalar(mean[:], avg[:], 1.0 / count, None, ALU.mult))
                    for t in range(tiles):
                        nc.vector.tensor_tensor(src[:, t], src[:, t], mean[:], ALU.subtract).then_inc(centered, 1)
                    dve.wait_ge(centered, tiles)

                def spread(g):
                    dve.wait_ge(rooted, g + 1)
                    link(nc.vector.reciprocal(inv[:, g % 2], var[:, g % 2]))
                    for t in range(g * size, g * size + size):
                        if weight is None:
                            ins = nc.vector.tensor_tensor(dst[:, t], src[:, t], inv[:, g % 2], ALU.mult)
                        else:
                            ins = nc.vector.scalar_tensor_tensor(out=dst[:, t], in0=src[:, t], scalar=weight(t),
                                                                 in1=inv[:, g % 2], op0=ALU.mult, op1=ALU.mult)
                        link(ins)
                        if bias is not None:
                            link(nc.vector.tensor_scalar(dst[:, t], dst[:, t], bias(t), None, ALU.add))
                        if times is not None:
                            link(nc.vector.tensor_tensor(dst[:, t], dst[:, t], times[:, t], ALU.mult))
                        if mod is not None:
                            layer, part = mod
                            nc.vector.tensor_scalar(C.H[:, t], dst[:, t], C.m(layer, part + 1, t), C.m(layer, part, t),
                                                    ALU.mult, ALU.add)
                for g in range(groups):
                    dve.wait_ge(summed, (g + 1) * size)
                    nc.vector.tensor_scalar(var[:, g % 2], acc[:, g % 2], 1.0 / count, eps, ALU.mult, ALU.add
                                            ).then_inc(sqrt_in, 1)
                    if g >= 1:
                        spread(g - 1)
                spread(groups - 1)



def attention_phase(nc, io, C, out):
    with Phase(nc, "attn") as ph:
        w_loaded = [ph.sem(f"w_loaded{n}") for n in range(3)]
        (projected, qk_kept, v_kept, scored, score_read, max_ready, exp_done, mixed, turned, turn_kept,
         o_ready, head_done) = (ph.sem(n) for n in (
            "projected", "qk_kept", "v_kept", "scored", "score_read", "max_ready", "exp_done", "mixed",
            "turned", "turn_kept", "o_ready", "head_done"))
        chain_s = ph.sem("chain")
        w = ph.sb("w", [P, 3, KT, P])
        q, k = ph.sb("q", [P, S]), ph.sb("k", [P, S])
        v = ph.sb("v", [P, TB, P])
        e = ph.sb("e", [P, 8, S])
        a = ph.sb("a", [P, TB, S])
        tmp = ph.sb("tmp", [P, S])
        at = ph.sb("at", [P, TB, S])
        mx, nb, sums, rec = (ph.sb(n, [P, 8]) for n in ("mx", "nb", "sums", "rec"))
        proj = ph.ps("proj", [P, 3, S])
        sc = ph.ps("sc", [P, 4, S])
        tp = ph.ps("tp", [P, TB, P])
        SCALE = 0.125

        with ph.block() as block:
            @block.sync
            def _(sp):
                with sp.Fori(0, HEADS_DA) as i:
                    for n, t in enumerate((T_Q, T_K, T_V)):
                        sp.wait_ge(projected, 3 * i)
                        sp.dma_start(w[:, n], w_tile(io["w_in"], i + t)).then_inc(w_loaded[n], 16)

            @block.tensor
            def _(pe):
                def scores(i, qb):
                    n = (qb + 1) * P
                    for j in range(2):
                        u = 2 * qb + j
                        pe.wait_ge(score_read, 8 * i + u + 1)
                        r = slice(64 * j, 64 * j + 64)
                        nc.tensor.matmul(sc[:, u % 4, 0:n], q[r, qb * P:n], k[r, 0:n], start=True, stop=True
                                         ).then_inc(scored, 1)

                def turn(i, qb):
                    pe.wait_ge(mixed, 4 * i + qb + 1)
                    pe.wait_ge(turn_kept, 4 * i + qb)
                    for kb in range(qb + 1):
                        last = nc.tensor.transpose(tp[:, kb], a[:, qb, kb * P:(kb + 1) * P], C.ident[:])
                    last.then_inc(turned, 1)

                def project_qk(i, n):
                    pe.wait_ge(w_loaded[n], 16 * (i + 1))
                    pe.wait_ge(qk_kept, 2 * i)
                    product(nc, proj[:, n], w[:, n], C.H, KT).then_inc(projected, 1)

                def project_v(i):
                    pe.wait_ge(w_loaded[2], 16 * (i + 1))
                    pe.wait_ge(v_kept, i + 0)
                    for tb in range(TB):
                        for kk in range(KT):
                            last = nc.tensor.matmul(proj[:, 2, tb * P:(tb + 1) * P], C.H[:, kk, tb * P:(tb + 1) * P],
                                                    w[:, 2, kk], start=(kk == 0), stop=(kk == KT - 1))
                    last.then_inc(projected, 1)

                def head(i, more):
                    pe.wait_ge(qk_kept, 2 * i + 2)
                    scores(i, 0)
                    scores(i, 1)
                    if more:
                        project_qk(i + 1, 0)
                    pe.wait_ge(head_done, i + 0)
                    turn(i, 0)
                    scores(i, 2)
                    if more:
                        project_qk(i + 1, 1)
                    turn(i, 1)
                    scores(i, 3)
                    if more:
                        pe.wait_ge(v_kept, i + 1)
                        project_v(i + 1)
                    turn(i, 2)
                    turn(i, 3)
                    pe.wait_ge(turn_kept, 4 * i + 4)
                    pe.wait_ge(v_kept, i + 1)
                    for kb in range(TB):
                        last = nc.tensor.matmul(tp[:].rearrange("p a n -> p (a n)")[:, kb * P:S], v[:, kb],
                                                at[:, kb, kb * P:S], start=(kb == 0), stop=(kb == TB - 1))
                    last.then_inc(o_ready, 1)

                project_qk(0, 0)
                project_qk(0, 1)
                project_v(0)
                with pe.Fori(0, HEADS_DA - 1) as i:
                    head(i, True)
                head(HEADS_DA - 1, False)

            @block.scalar
            def _(act):
                def exps(i, qb):
                    n = (qb + 1) * P
                    for j in range(2):
                        u = 2 * qb + j
                        act.wait_ge(max_ready, 8 * i + u + 1)
                        nc.scalar.activation(e[:, u, 0:n], e[:, u, 0:n], ACT.Exp, bias=nb[:, u:u + 1], scale=SCALE,
                                             accum_out=sums[:, u:u + 1]).then_inc(exp_done, 1)

                def keep_turn(i, qb):
                    act.wait_ge(turned, 4 * i + qb + 1)
                    nc.scalar.activation(at[:, 0:qb + 1, qb * P:(qb + 1) * P], tp[:, 0:qb + 1], ACT.Copy
                                         ).then_inc(turn_kept, 1)

                with act.Fori(0, HEADS_DA) as i:
                    act.wait_ge(projected, 3 * i + 1)
                    nc.scalar.activation(q[:], proj[:, 0], ACT.Copy).then_inc(qk_kept, 1)
                    act.wait_ge(projected, 3 * i + 2)
                    nc.scalar.activation(k[:], proj[:, 1], ACT.Copy).then_inc(qk_kept, 1)
                    act.wait_ge(head_done, i + 0)
                    exps(i, 0)
                    exps(i, 1)
                    keep_turn(i, 0)
                    exps(i, 2)
                    keep_turn(i, 1)
                    exps(i, 3)
                    keep_turn(i, 2)
                    keep_turn(i, 3)

            @block.vector
            def _(dve):
                link = Chain(dve, chain_s)

                def scale_and_max(i, qb):
                    n = (qb + 1) * P
                    for j in range(2):
                        u = 2 * qb + j
                        dve.wait_ge(scored, 8 * i + u + 1)
                        nc.vector.scalar_tensor_tensor(out=e[:, u, 0:n], in0=C.dist[:, S - n:S],
                                                       scalar=C.nslope[:, ds(i, 1)], in1=sc[:, u % 4, 0:n],
                                                       op0=ALU.mult, op1=ALU.add).then_inc(score_read, 1)
                        dve.wait_ge(score_read, 8 * i + u + 5)
                        link(nc.vector.reduce_max(mx[:, u:u + 1], e[:, u, 0:n], AX_X))
                        nc.vector.tensor_scalar(nb[:, u:u + 1], mx[:, u:u + 1], -SCALE, None, ALU.mult
                                                ).then_inc(max_ready, 1)

                def difference(i, qb):
                    n = (qb + 1) * P
                    dve.wait_ge(exp_done, 8 * i + 2 * qb + 2)
                    r = rec[:, 2 * qb:2 * qb + 2]
                    link(nc.vector.reciprocal(r, sums[:, 2 * qb:2 * qb + 2]))
                    link(nc.vector.tensor_tensor(r[:, 1:2], r[:, 1:2], C.nlam[:], ALU.mult))
                    link(nc.vector.tensor_scalar(tmp[:, 0:n], e[:, 2 * qb + 1, 0:n], r[:, 1:2], None, ALU.mult))
                    nc.vector.scalar_tensor_tensor(out=a[:, qb, 0:n], in0=e[:, 2 * qb, 0:n], scalar=r[:, 0:1],
                                                   in1=tmp[:, 0:n], op0=ALU.mult, op1=ALU.add).then_inc(mixed, 1)
                    dve.wait_ge(mixed, 4 * i + qb + 1)

                dve.sem_inc(score_read, 4)
                with dve.Fori(0, HEADS_DA) as i:
                    link.restart()
                    dve.wait_ge(projected, 3 * i + 3)
                    nc.vector.tensor_copy(v[:].rearrange("p a n -> p (a n)"), proj[:, 2]).then_inc(v_kept, 1)
                    scale_and_max(i, 0)
                    scale_and_max(i, 1)
                    difference(i, 0)
                    scale_and_max(i, 2)
                    difference(i, 1)
                    scale_and_max(i, 3)
                    difference(i, 2)
                    difference(i, 3)
                    dve.wait_ge(o_ready, i + 1)
                    nc.vector.tensor_copy(tile_at(out, i), tp[:].rearrange("p a n -> p (a n)")).then_inc(head_done, 1)
    norm_phase(nc, C, "subln", out, out, HEADS_DA, 1, P, EPS_LN, weight=lambda t: C.subln[:])


def projection_phase(nc, name, weights, first, count, ring, src, kt, epilogue, spaces=(), engine="scalar"):
    with Phase(nc, name) as ph:
        loaded = [ph.sem(f"loaded{r}") for r in range(ring)]
        projected, kept, epi = ph.sem("projected"), ph.sem("kept"), ph.sem("epilogue")
        w = ph.sb("w", [P, ring, kt, P])
        extra = [ph.sb(n, shape) for n, shape in spaces]
        acc = ph.ps("acc", [P, ring, S])
        with ph.block() as block:
            @block.sync
            def _(sp):
                with sp.Fori(0, count // ring) as i:
                    for r in range(ring):
                        sp.wait_ge(projected, ring * i + r + 1)
                        sp.dma_start(w[:, r], w_tile(weights, i * ring + (first + r))).then_inc(loaded[r], 16)

            @block.tensor
            def _(pe):
                pe.sem_inc(projected, ring)
                with pe.Fori(0, count // ring) as i:
                    for r in range(ring):
                        pe.wait_ge(loaded[r], 16 * (i + 1))
                        pe.wait_ge(kept, ring * i + r + 1)
                        product(nc, acc[:, r], w[:, r], src, kt).then_inc(projected, 1)

            def keep(eng, chain):
                eng.sem_inc(kept, ring)
                with eng.Fori(0, count // ring) as i:
                    chain.restart()
                    for r in range(ring):
                        eng.wait_ge(projected, ring * i + r + 1 + ring)
                        epilogue(chain, i, r, acc[:, r], *extra).then_inc(kept, 1)

            if engine == "scalar":
                @block.scalar
                def _(act):
                    keep(act, Chain(act, epi))
            else:
                @block.vector
                def _(dve):
                    keep(dve, Chain(dve, epi))


def conv_silu_front(nc, dve, link, u, x, taps, bias, col):
    link(nc.vector.tensor_scalar(x, u[:, 0:S], taps(0, col), bias(col), ALU.mult, ALU.add))
    for n in range(1, 4):
        ins = nc.vector.scalar_tensor_tensor(out=x, in0=u[:, n:n + S], scalar=taps(n, col), in1=x,
                                             op0=ALU.mult, op1=ALU.add)
        if n < 3:
            link(ins)
    return ins


CB_AT = [0, 512, 896, 1152]
CB_LEN = 1280


def cb_slice(sb):
    return slice(CB_AT[sb], CB_AT[sb] + S - sb * P)


def ssd_setup_phase(nc, io, C, cb, cumc, dtc):
    with Phase(nc, "ssdset") as ph:
        names = ("w_loaded", "dt_loaded", "projected", "u_kept", "conv_done", "x_ready", "dt_projected", "abs_ready",
                 "ln_ready", "cum_ready", "turned", "stored", "cb_ready", "cb_kept", "a_ready")
        (w_loaded, dt_loaded, projected, u_kept, conv_done, x_ready, dt_projected, abs_ready, ln_ready, cum_ready,
         turned, stored, cb_ready, cb_kept, a_ready) = (ph.sem(n) for n in names)
        chain_s, chain2_s, zero_s = ph.sem("chain"), ph.sem("chain2"), ph.sem("zeroed")
        w = ph.sb("w", [P, KT, P])
        wdt = ph.sb("wdt", [P, KT, 32])
        u = ph.sb("u", [P, S + 3])
        bc = ph.sb("bc", [P, 8, S])
        pre = ph.sb("pre", [P, S])
        t0, t1, dt, cum, one = (ph.sb(n, [32, S]) for n in ("t0", "t1", "dt", "cum", "one"))
        na = ph.sb("na", [32, 1])
        proj = ph.ps("proj", [P, S])
        dps = ph.ps("dps", [P, S])
        tps = ph.ps("tps", [P, 2, TB, 32])
        cps = ph.ps("cps", [P, 2, S])
        TILES = 8
        with ph.block() as block:
            @block.sync
            def _(sp):
                sp.dma_start(wdt[:], io["w_dt"]).then_inc(dt_loaded, 16)
                with sp.Fori(0, TILES) as i:
                    sp.wait_ge(projected, i + 0)
                    sp.dma_start(w[:], w_tile(io["w_in"], i + T_B)).then_inc(w_loaded, 16)
                sp.wait_ge(cum_ready, 2)
                sp.dma_start(io["cum"], cum[:]).then_inc(stored, 16)
                sp.wait_ge(stored, 16)

            @block.tensor
            def _(pe):
                pe.wait_ge(dt_loaded, 16)
                product(nc, dps[0:32], wdt, C.H, KT).then_inc(dt_projected, 1)
                with pe.Fori(0, TILES) as i:
                    pe.wait_ge(w_loaded, 16 * (i + 1))
                    pe.wait_ge(u_kept, i + 0)
                    product(nc, proj[:], w, C.H, KT).then_inc(projected, 1)
                pe.wait_ge(cum_ready, 2)
                for n, src in enumerate((cum, dt)):
                    for tb in range(TB):
                        last = nc.tensor.transpose(tps[:, n, tb], src[:, tb * P:(tb + 1) * P], C.ident[0:32, 0:32])
                last.then_inc(turned, 1)
                pe.wait_ge(x_ready, TILES)
                for g in range(SSD_GROUPS):
                    for sb in range(TB):
                        n = g * TB + sb
                        if n >= 2:
                            pe.wait_ge(cb_kept, n - 1)
                        nc.tensor.matmul(cps[:, n % 2, 0:S - sb * P], bc[:, g, sb * P:(sb + 1) * P],
                                         bc[:, 4 + g, sb * P:S], start=True, stop=True).then_inc(cb_ready, 1)

            @block.scalar
            def _(act):
                act.wait_ge(abs_ready, 1)
                nc.scalar.activation(t1[:], t1[:], ACT.Exp, scale=-1.0).then_inc(ln_ready, 1)
                nc.scalar.activation(na[:], C.v("head_ssd", 1)[0:32], ACT.Exp).then_inc(a_ready, 1)
                act.wait_ge(ln_ready, 1)
                act.wait_ge(abs_ready, 2)
                nc.scalar.activation(t1[:], t1[:], ACT.Ln).then_inc(ln_ready, 1)
                with act.Fori(0, TILES) as i:
                    act.wait_ge(projected, i + 1)
                    act.wait_ge(conv_done, i + 1)
                    nc.scalar.activation(u[:, 3:], proj[:], ACT.Copy).then_inc(u_kept, 1)
                    act.wait_ge(conv_done, i + 2)
                    nc.scalar.activation(tile_at(bc, i), pre[:], ACT.Silu).then_inc(x_ready, 1)
                act.wait_ge(turned, 1)
                nc.scalar.activation(cumc[:], tps[:, 0], ACT.Copy)
                nc.scalar.activation(dtc[:], tps[:, 1], ACT.Copy)

            @block.vector
            def _(dve):
                link = Chain(dve, chain_s)
                nc.vector.memset(u[:, 0:3], 0.0).then_inc(conv_done, 1)
                link(nc.vector.memset(one[:], 1.0))
                dve.wait_ge(dt_projected, 1)
                link(nc.vector.tensor_scalar(t0[:], dps[0:32], C.v("head_ssd", 0)[0:32], None, ALU.add))
                nc.vector.scalar_tensor_tensor(out=t1[:], in0=t0[:], scalar=-1.0, in1=t0[:], op0=ALU.mult, op1=ALU.max
                                               ).then_inc(abs_ready, 1)
                dve.wait_ge(ln_ready, 1)
                nc.vector.tensor_scalar(t1[:], t1[:], 1.0, None, ALU.add).then_inc(abs_ready, 1)
                dve.wait_ge(ln_ready, 2)
                nc.vector.scalar_tensor_tensor(out=dt[:], in0=t0[:], scalar=0.0, in1=t1[:], op0=ALU.max, op1=ALU.add
                                               ).then_inc(cum_ready, 1)
                dve.wait_ge(cum_ready, 1)
                dve.wait_ge(a_ready, 1)
                link(nc.vector.tensor_scalar(t0[:], dt[:], na[:], -1.0, ALU.mult, ALU.mult))
                nc.vector.tensor_tensor_scan(cum[:], one[:], t0[:], 0.0, ALU.mult, ALU.add).then_inc(cum_ready, 1)
                link2 = Chain(dve, chain2_s)
                with dve.Fori(0, TILES) as i:
                    link2.restart()
                    dve.wait_ge(u_kept, i + 1)
                    dve.wait_ge(x_ready, i + 0)
                    conv_silu_front(nc, dve, link2, u, pre[:], lambda n, c: C.v(f"conv_w{n}", c),
                                    lambda c: C.v("conv_b", c), i + 16).then_inc(conv_done, 1)
                for n in range(SSD_GROUPS * TB):
                    g, sb = n // TB, n % TB
                    dve.wait_ge(cb_ready, n + 1)
                    at = CB_AT[sb]
                    link(nc.vector.tensor_tensor(cb[:, g, at:at + P], cps[:, n % 2, 0:P], C.keep[:], ALU.mult))
                    if sb < TB - 1:
                        nc.vector.tensor_copy(cb[:, g, at + P:at + S - sb * P], cps[:, n % 2, P:S - sb * P]
                                              ).then_inc(cb_kept, 1)
                    else:
                        dve.sem_inc(cb_kept, 1)


def decay_weights(nc, dve, e, rows, col):
    for sb in range(TB):
        last = nc.vector.tensor_scalar(e[:, cb_slice(sb)], rows[:, sb * P:S], col(sb), 0.0, ALU.subtract, ALU.min)
    return last


def ssd_phase(nc, io, C, out, cb, cumc, dtc):
    with Phase(nc, "ssd") as ph:
        wx_loaded, wz_loaded, rows_loaded = ph.sem("wx_loaded"), ph.sem("wz_loaded"), ph.sem("rows_loaded")
        names = ("projected", "kept", "conv_done", "x_ready", "turned", "turn_kept", "shifted", "exp_done", "weighted",
                 "y_ready", "tile_done", "zeroed")
        (projected, kept, conv_done, x_ready, turned, turn_kept, shifted, exp_done, weighted, y_ready, tile_done,
         zeroed) = (ph.sem(n) for n in names)
        chain_s = ph.sem("chain")
        wx, wz = ph.sb("wx", [P, KT, P]), ph.sb("wz", [P, KT, P])
        rows = ph.sb("rows", [P, 2, S])
        u = ph.sb("u", [P, S + 3])
        pre, x, z = ph.sb("pre", [P, S]), ph.sb("x", [P, S]), ph.sb("z", [P, S])
        xt = ph.sb("xt", [P, TB, P])
        e = ph.sb("e", [P, 2, CB_LEN])
        wt = ph.sb("wt", [P, 2, CB_LEN])
        y = ph.sb("y", [P, S])
        proj = ph.ps("proj", [P, 2, S])
        tp = ph.ps("tp", [P, TB, P])
        yp = ph.ps("yp", [P, S])
        LAST = SSD_TILES - 1

        with ph.block() as block:
            @block.sync
            def _(sp):
                with sp.Fori(0, SSD_TILES) as i:
                    sp.wait_ge(projected, 2 * i)
                    sp.dma_start(wx[:], w_tile(io["w_in"], i + T_XS)).then_inc(wx_loaded, 16)
                    sp.dma_start(wz[:], w_tile(io["w_in"], i + T_Z)).then_inc(wz_loaded, 16)
                    sp.wait_ge(shifted, 2 * i)
                    for h in range(2):
                        sp.dma_start(rows[:, h], io["cum"][ds(2 * i + h, 1)].broadcast_to([P, S])
                                     ).then_inc(rows_loaded, 16)

            @block.tensor
            def _(pe):
                def project(i):
                    pe.wait_ge(wx_loaded, 16 * (i + 1))
                    pe.wait_ge(kept, 2 * i)
                    product(nc, proj[:, 0], wx, C.H, KT).then_inc(projected, 1)
                    pe.wait_ge(wz_loaded, 16 * (i + 1))
                    product(nc, proj[:, 1], wz, C.H, KT).then_inc(projected, 1)

                def apply(i):
                    pe.wait_ge(x_ready, i + 1)
                    pe.wait_ge(turn_kept, i + 0)
                    for tb in range(TB):
                        last = nc.tensor.transpose(tp[:, tb], x[:, tb * P:(tb + 1) * P], C.ident[:])
                    last.then_inc(turned, 1)
                    pe.wait_ge(turn_kept, i + 1)
                    pe.wait_ge(tile_done, i + 0)
                    for h in range(2):
                        r = slice(64 * h, 64 * h + 64)
                        pe.wait_ge(weighted, 2 * i + h + 1)
                        for sb in range(TB):
                            last = nc.tensor.matmul(yp[r, sb * P:S], xt[:, sb, r], wt[:, h, cb_slice(sb)],
                                                    start=(sb == 0), stop=(sb == TB - 1))
                    last.then_inc(y_ready, 1)

                project(0)
                with pe.Fori(0, LAST) as i:
                    project(i + 1)
                    apply(i)
                apply(LAST)

            @block.scalar
            def _(act):
                with act.Fori(0, SSD_TILES) as i:
                    act.wait_ge(conv_done, i + 1)
                    act.wait_ge(projected, 2 * i + 1)
                    nc.scalar.activation(u[:, 3:], proj[:, 0], ACT.Copy).then_inc(kept, 1)
                    act.wait_ge(projected, 2 * i + 2)
                    act.wait_ge(tile_done, i + 0)
                    nc.scalar.activation(z[:], proj[:, 1], ACT.Silu).then_inc(kept, 1)
                    act.wait_ge(conv_done, i + 2)
                    nc.scalar.activation(x[:], pre[:], ACT.Silu).then_inc(x_ready, 1)
                    for h in range(2):
                        act.wait_ge(shifted, 2 * i + h + 1)
                        nc.scalar.activation(e[:, h], e[:, h], ACT.Exp).then_inc(exp_done, 1)
                    act.wait_ge(turned, i + 1)
                    nc.scalar.activation(xt[:], tp[:], ACT.Copy).then_inc(turn_kept, 1)

            @block.vector
            def _(dve):
                nc.vector.memset(u[:, 0:3], 0.0).then_inc(conv_done, 1)
                link = Chain(dve, chain_s)
                with dve.Fori(0, SSD_GROUPS) as g:
                    with dve.Fori(0, 4) as j:
                        i = dve.snap(g * 4 + j)
                        link.restart()
                        dve.wait_ge(kept, 2 * i + 1)
                        dve.wait_ge(x_ready, i + 0)
                        conv_silu_front(nc, dve, link, u, pre[:], lambda n, c: C.v(f"conv_w{n}", c),
                                        lambda c: C.v("conv_b", c), i).then_inc(conv_done, 1)
                        dve.wait_ge(rows_loaded, 32 * (i + 1))
                        for h in range(2):
                            decay_weights(nc, dve, e[:, h], rows[:, h],
                                          lambda sb: cumc[:, sb, ds(2 * i + h, 1)]).then_inc(shifted, 1)
                        for h in range(2):
                            dve.wait_ge(exp_done, 2 * i + h + 1)
                            for sb in range(TB):
                                last = nc.vector.scalar_tensor_tensor(
                                    out=wt[:, h, cb_slice(sb)], in0=e[:, h, cb_slice(sb)],
                                    scalar=dtc[:, sb, ds(2 * i + h, 1)],
                                    in1=cb[:, ds(g, 1), cb_slice(sb)].rearrange("p a n -> p (a n)"),
                                    op0=ALU.mult, op1=ALU.mult)
                            last.then_inc(weighted, 1)
                        dve.wait_ge(y_ready, i + 1)
                        dve.wait_ge(x_ready, i + 1)
                        link(nc.vector.scalar_tensor_tensor(out=y[:], in0=x[:], scalar=C.v("d_skip", i), in1=yp[:],
                                                            op0=ALU.mult, op1=ALU.add))
                        dve.wait_ge(kept, 2 * i + 2)
                        link(nc.vector.tensor_tensor(tile_at(out, i), y[:], z[:], ALU.mult))
                        dve.sem_inc(tile_done, 1)
    norm_phase(nc, C, "ssdnorm", out, out, SSD_GROUPS, 4, 4 * P, EPS_LN, weight=lambda t: C.v("ssd_norm", t))


def mix_phase(nc, io, C, attn, ssd, mixed):
    with Phase(nc, "mix") as ph:
        loaded = [ph.sem(f"loaded{n}") for n in range(4)]
        projected, gated, kept, chain_s, done = (ph.sem(n) for n in ("projected", "gated", "kept", "chain", "done"))
        w = [ph.sb(f"w{n}", [P, kt, P]) for n, kt in enumerate((8, 8, 8, 16))]
        gate = ph.sb("gate", [P, 2, S])
        half = ph.sb("half", [P, 2, S])
        acc = ph.ps("acc", [P, 4, S])
        sources = ((io["w_in"], T_GA, C.H, 8), (io["w_in"], T_GS, C.H, 8), (io["w_attn_branch"], 0, attn, 8),
                   (io["w_ssd_branch"], 0, ssd, 16))
        with ph.block() as block:
            @block.sync
            def _(sp):
                with sp.Fori(0, KT) as i:
                    for n, (weights, first, _, _) in enumerate(sources):
                        sp.wait_ge(projected, 4 * i + n + 1)
                        sp.dma_start(w[n][:], w_tile(weights, i + first)).then_inc(loaded[n], 16)

            @block.tensor
            def _(pe):
                pe.sem_inc(projected, 4)
                with pe.Fori(0, KT) as i:
                    for n, (_, _, src, kt) in enumerate(sources):
                        pe.wait_ge(loaded[n], 16 * (i + 1))
                        pe.wait_ge(gated if n < 2 else kept, 2 * i + n % 2 + 1)
                        product(nc, acc[:, n], w[n], src, kt).then_inc(projected, 1)

            @block.scalar
            def _(act):
                act.sem_inc(gated, 2)
                with act.Fori(0, KT) as i:
                    for n in range(2):
                        act.wait_ge(projected, 4 * i + n + 5)
                        act.wait_ge(kept, 2 * i + n + 1)
                        nc.scalar.activation(gate[:, n], acc[:, n], ACT.Sigmoid).then_inc(gated, 1)

            @block.vector
            def _(dve):
                dve.sem_inc(kept, 2)
                with dve.Fori(0, KT) as i:
                    for n in range(2):
                        dve.wait_ge(projected, 4 * i + n + 7)
                        dve.wait_ge(gated, 2 * i + n + 3)
                        if n == 0:
                            dve.wait_ge(done, i + 0)
                        nc.vector.tensor_tensor(half[:, n], gate[:, n], acc[:, 2 + n], ALU.mult).then_inc(kept, 1)
                    dve.wait_ge(kept, 2 * i + 4)
                    nc.vector.tensor_tensor(tile_at(mixed, i), half[:, 0], half[:, 1], ALU.add).then_inc(done, 1)


def gated_residual(nc, C, layer, part, alpha):
    def epilogue(ring):
        def run(chain, i, r, bank, tmp):
            t = i * ring + r
            x = tile_at(C.X, t)
            col = 48 * layer + 8 * part
            chain(nc.vector.tensor_scalar(tmp[:, r], bank, C.mod[:, ds(t + col, 1)], None, ALU.mult))
            return nc.vector.scalar_tensor_tensor(out=x, in0=x, scalar=alpha, in1=tmp[:, r], op0=ALU.mult, op1=ALU.add)
        return run
    return epilogue


def residual_projection(nc, C, name, weights, src, kt, layer, part, alpha, ring=2):
    projection_phase(nc, name, weights, 0, KT, ring, src, kt, gated_residual(nc, C, layer, part, alpha)(ring),
                     spaces=(("tmp", [P, ring, S]),), engine="vector")


def first_block(nc, io, C):
    setup_phase(nc, io, C)
    ada_phase(nc, io, C)
    modulate_phase(nc, C, 0, 0)
    with ExitStack() as ctx:
        def sb(name, shape):
            return ctx.enter_context(nc.sbuf_tensor(name, shape, F32))
        attn = sb("attn_out", [P, KT, S])
        attention_phase(nc, io, C, attn)
        ssd = sb("ssd_out", [P, SSD_TILES, S])
        with ExitStack() as inner:
            cb = inner.enter_context(nc.sbuf_tensor("cb", [P, SSD_GROUPS, CB_LEN], F32))
            cumc = inner.enter_context(nc.sbuf_tensor("cumc", [P, TB, SSD_HEADS], F32))
            dtc = inner.enter_context(nc.sbuf_tensor("dtc", [P, TB, SSD_HEADS], F32))
            ssd_setup_phase(nc, io, C, cb, cumc, dtc)
            ssd_phase(nc, io, C, ssd, cb, cumc, dtc)
        mixed = sb("mixed", [P, KT, S])
        mix_phase(nc, io, C, attn, ssd, mixed)
        residual_projection(nc, C, "out1", io["w_out"], mixed, KT, 0, 2, ALPHA)
    norm_phase(nc, C, "ln1", C.X, C.X, 1, KT, D, EPS_LN, weight=lambda t: C.v("ln1_g", t),
               bias=lambda t: C.v("ln1_b", t), center=True, mod=(0, 3))
    peer_block(nc, io, C)



HEADS_PEER, TOPK = 8, 16


def top16(nc, link, values, work, best, index):
    link(nc.vector.max(best[:, 0:8], values))
    link(nc.vector.match_replace(work, best[:, 0:8], values, -1e30))
    link(nc.vector.max(best[:, 8:16], work))
    link(nc.vector.max_index(index[:, 0:8], best[:, 0:8], values))
    link(nc.vector.max_index(index[:, 8:16], best[:, 8:16], work))


def peer_select_phase(nc, io, C, sel):
    with Phase(nc, "select") as ph:
        w_loaded, keys_loaded = [ph.sem(f"w_loaded{n}") for n in range(2)], ph.sem("keys_loaded")
        names = ("projected", "q_kept", "scored", "score_kept", "selected", "turned", "turn_kept", "exp_in", "exp_out")
        (projected, q_kept, scored, score_kept, selected, turned, turn_kept, exp_in, exp_out) = (
            ph.sem(n) for n in names)
        chain_s = ph.sem("chain")
        w = ph.sb("w", [P, 2, KT, P])
        keys = ph.sb("keys", [P, 2, P])
        q = ph.sb("q", [P, 2, S])
        s = ph.sb("s", [P, 2, TB, P])
        work = ph.sb("work", [P, P])
        best = ph.sb("best", [P, TB, 2, TOPK])
        index = ph.sb("index", [P, TB, 2, TOPK], U32)
        index_f = ph.sb("index_f", [P, TB, 2, TOPK])
        pairs = ph.sb("pairs", [P, TB, TOPK, TOPK])
        pwork = ph.sb("pwork", [P, TOPK * TOPK])
        top, soft = ph.sb("top", [P, TB, TOPK]), ph.sb("soft", [P, TB, TOPK])
        where = ph.sb("where", [P, TB, TOPK], U32)
        rank = ph.sb("rank", [P, 2, TB, TOPK], U32)
        rank_f = ph.sb("rank_f", [P, 2, TB, TOPK])
        total = ph.sb("total", [P, TB])
        chosen = ph.sb("chosen", [P, TB, 3, HEADS_PEER * TOPK])
        proj = ph.ps("proj", [P, 2, S])
        sc = ph.ps("sc", [P, 2, TB, P])
        tp = ph.ps("tp", [P, 3, TB, P])
        LAST = HEADS_PEER - 1

        with ph.block() as block:
            @block.sync
            def _(sp):
                sp.dma_start(keys[:], io["keys"]).then_inc(keys_loaded, 16)
                with sp.Fori(0, HEADS_PEER) as i:
                    for j in range(2):
                        sp.wait_ge(projected, 2 * i + j + 1)
                        sp.dma_start(w[:, j], w_tile(io["w_query"], 2 * i + j)).then_inc(w_loaded[j], 16)

            @block.tensor
            def _(pe):
                def project(i):
                    for j in range(2):
                        pe.wait_ge(w_loaded[j], 16 * (i + 1))
                        pe.wait_ge(q_kept, 2 * i)
                        product(nc, proj[:, j], w[:, j], C.H, KT).then_inc(projected, 1)

                def score(i):
                    pe.wait_ge(q_kept, 2 * i + 2)
                    pe.wait_ge(score_kept, 2 * i)
                    for j in range(2):
                        for tb in range(TB):
                            last = nc.tensor.matmul(sc[:, j, tb], q[:, j, tb * P:(tb + 1) * P], keys[:, j],
                                                    start=True, stop=True)
                        last.then_inc(scored, 1)
                pe.sem_inc(projected, 2)
                pe.wait_ge(keys_loaded, 16)
                project(0)
                with pe.Fori(0, LAST) as i:
                    score(i)
                    project(i + 1)
                score(LAST)
                pe.wait_ge(selected, HEADS_PEER)
                for n in range(3):
                    for tb in range(TB):
                        last = nc.tensor.transpose(tp[:, n, tb], chosen[:, tb, n], C.ident[:])
                    last.then_inc(turned, 1)

            @block.scalar
            def _(act):
                with act.Fori(0, HEADS_PEER) as i:
                    for j in range(2):
                        act.wait_ge(projected, 2 * i + j + 3)
                        act.wait_ge(scored, 2 * i)
                        nc.scalar.activation(q[:, j], proj[:, j], ACT.Copy).then_inc(q_kept, 1)
                    act.wait_ge(selected, i + 0)
                    for j in range(2):
                        act.wait_ge(scored, 2 * i + j + 1)
                        nc.scalar.activation(s[:, j], sc[:, j], ACT.Copy).then_inc(score_kept, 1)
                    act.wait_ge(exp_in, i + 1)
                    nc.scalar.activation(soft[:], soft[:], ACT.Exp).then_inc(exp_out, 1)
                for n in range(3):
                    act.wait_ge(turned, n + 1)
                    nc.scalar.activation(sel[:, n], tp[:, n], ACT.Copy)

            @block.vector
            def _(dve):
                link = Chain(dve, chain_s)
                grid = [P, TB, TOPK, TOPK]

                with dve.Fori(0, HEADS_PEER) as i:
                    link.restart()
                    for j in range(2):
                        dve.wait_ge(score_kept, 2 * i + j + 1)
                        link(nc.vector.memset(work[:, 0:1], 0.0))
                        for tb in range(TB):
                            top16(nc, link, s[:, j, tb], work[:], best[:, tb, j], index[:, tb, j])
                    link(nc.vector.tensor_copy(index_f[:], index[:]))
                    link(nc.vector.tensor_tensor(pairs[:], best[:, :, 0].unsqueeze(3).broadcast_to(grid),
                                                 best[:, :, 1].unsqueeze(2).broadcast_to(grid), ALU.add))
                    for tb in range(TB):
                        top16(nc, link, pairs[:, tb].rearrange("p a b -> p (a b)"), pwork[:], top[:, tb], where[:, tb])
                    link(nc.vector.tensor_scalar(rank[:, 0], where[:], 4, None, ALU.logical_shift_right))
                    link(nc.vector.tensor_scalar(rank[:, 1], where[:], 15, None, ALU.bitwise_and))
                    link(nc.vector.tensor_copy(rank_f[:], rank[:]))
                    nc.vector.tensor_tensor(soft[:], top[:], top[:, :, 0:1].broadcast_to([P, TB, TOPK]), ALU.subtract
                                            ).then_inc(exp_in, 1)
                    at = ds(i * TOPK, TOPK)
                    for j in range(2):
                        link(nc.vector.tensor_tensor(pairs[:], rank_f[:, j].unsqueeze(3).broadcast_to(grid),
                                                     C.iota[:, 0:TOPK].unsqueeze(1).unsqueeze(1).broadcast_to(grid),
                                                     ALU.is_equal))
                        link(nc.vector.tensor_tensor(pairs[:], pairs[:],
                                                     index_f[:, :, j].unsqueeze(2).broadcast_to(grid), ALU.mult))
                        link(nc.vector.reduce_sum(chosen[:, :, j, at], pairs[:], AX_X))
                    dve.wait_ge(exp_out, i + 1)
                    link(nc.vector.reduce_sum(total[:], soft[:], AX_X))
                    link(nc.vector.reciprocal(total[:], total[:]))
                    nc.vector.tensor_tensor(chosen[:, :, 2, at], soft[:],
                                            total[:].unsqueeze(2).broadcast_to([P, TB, TOPK]), ALU.mult
                                            ).then_inc(selected, 1)


def experts_phase(nc, io, C, sel):
    HALF = S // 2
    GROUP = 4
    for half in range(2):
        with Phase(nc, f"experts{half}") as ph:
            u_loaded, v_loaded = [ph.sem(f"u_loaded{r}") for r in range(2)], [ph.sem(f"v_loaded{r}") for r in range(2)]
            names = ("rows_ready", "crossed", "gates_kept", "u_done", "gelu_done", "weighted", "v_done", "zeroed")
            rows_ready, crossed, gates_kept, u_done, gelu_done, weighted, v_done, zeroed = (ph.sem(n) for n in names)
            chain_s = ph.sem("chain")
            gates = ph.sb("gates", [P, P, HALF])
            t0 = half * HALF
            with ExitStack() as inner:
                first = inner.enter_context(nc.sbuf_tensor(f"first{half}", [P, 2 * GROUP, P], F32))
                second = inner.enter_context(nc.sbuf_tensor(f"second{half}", [P, 2 * GROUP, P], F32))
                cross = inner.enter_context(nc.psum_tensor(f"cross{half}", [P, 2, GROUP, P], F32))
                with ph.block() as block:
                    @block.vector
                    def _(dve):
                        dve.sem_inc(crossed, 2)
                        with dve.Fori(0, HALF // (2 * GROUP)) as i:
                            for b in range(2):
                                dve.wait_ge(crossed, 2 * i + b + 1)
                                for r in range(GROUP):
                                    t = i * (2 * GROUP) + (t0 + b * GROUP + r)
                                    n = b * GROUP + r
                                    nc.vector.tensor_scalar(first[:, n], C.iota[:], sel[:, 0, ds(t, 1)],
                                                            sel[:, 2, ds(t, 1)], ALU.is_equal, ALU.mult)
                                    last = nc.vector.tensor_scalar(second[:, n], C.iota[:], sel[:, 1, ds(t, 1)],
                                                                   None, ALU.is_equal)
                                last.then_inc(rows_ready, 1)

                    @block.tensor
                    def _(pe):
                        with pe.Fori(0, HALF // (2 * GROUP)) as i:
                            for b in range(2):
                                pe.wait_ge(rows_ready, 2 * i + b + 1)
                                pe.wait_ge(gates_kept, 2 * i + b + 1)
                                for r in range(GROUP):
                                    n = b * GROUP + r
                                    last = nc.tensor.matmul(cross[:, b, r], second[:, n], first[:, n],
                                                            start=True, stop=True)
                                last.then_inc(crossed, 1)

                    @block.scalar
                    def _(act):
                        act.sem_inc(gates_kept, 2)
                        by_token = gates[:].rearrange("p i t -> p t i")
                        with act.Fori(0, HALF // (2 * GROUP)) as i:
                            for b in range(2):
                                act.wait_ge(crossed, 2 * i + b + 3)
                                nc.scalar.activation(by_token[:, ds(i * (2 * GROUP) + b * GROUP, GROUP)],
                                                     cross[:, b], ACT.Copy).then_inc(gates_kept, 1)

            u, v = ph.sb("u", [P, 2, KT, P]), ph.sb("v", [P, 2, D])
            act_sb, wts = ph.sb("act", [P, 2, HALF]), ph.sb("wts", [P, 2, HALF])
            zero = ph.sb("zero", [P, S])
            scores = ph.ps("scores", [P, 2, S])
            y = ph.ps("y", [P, KT, HALF])
            with ph.block() as block:
                @block.sync
                def _(sp):
                    with sp.Fori(0, P // 2) as i:
                        for r in range(2):
                            sp.wait_ge(u_done, 2 * i + r + 1)
                            sp.dma_start(u[:, r], w_tile(io["u"], 2 * i + r)).then_inc(u_loaded[r], 16)
                            sp.wait_ge(v_done, 2 * i + r + 1)
                            sp.dma_start(v[:, r], io["v"][ds(2 * i + r, 1)].rearrange("a p n -> (a p) n")
                                         ).then_inc(v_loaded[r], 16)

                @block.tensor
                def _(pe):
                    def scores_of(i, r):
                        pe.wait_ge(u_loaded[r], 16 * (i + 1))
                        pe.wait_ge(gelu_done, 2 * i + r + 1)
                        for k in range(KT):
                            last = nc.tensor.matmul(scores[:, r, 0:HALF], u[:, r, k], C.H[:, k, t0:t0 + HALF],
                                                    start=(k == 0), stop=(k == KT - 1))
                        last.then_inc(u_done, 1)

                    def add_values(i, r):
                        pe.wait_ge(v_loaded[r], 16 * (i + 1))
                        pe.wait_ge(weighted, 2 * i + r + 3)
                        for k in range(KT):
                            last = nc.tensor.matmul(y[:, k], v[:, r, k * P:(k + 1) * P], wts[:, r], start=False,
                                                    stop=False, skip_group_check=True)
                        last.then_inc(v_done, 1)

                    pe.sem_inc(u_done, 2)
                    pe.sem_inc(v_done, 2)
                    pe.wait_ge(zeroed, 1)
                    for k in range(0, KT, 2):
                        nc.tensor.matmul(y[:, k:k + 2].rearrange("p a n -> p (a n)"), C.ones[:],
                                         zero[:], start=True, stop=False, skip_group_check=True)
                    scores_of(0, 0)
                    with pe.Fori(0, P // 2 - 1) as i:
                        scores_of(i, 1)
                        add_values(i, 0)
                        scores_of(i + 1, 0)
                        add_values(i, 1)
                    scores_of(P // 2 - 1, 1)
                    add_values(P // 2 - 1, 0)
                    add_values(P // 2 - 1, 1)

                @block.scalar
                def _(act):
                    act.sem_inc(gelu_done, 2)
                    with act.Fori(0, P // 2) as i:
                        for r in range(2):
                            act.wait_ge(u_done, 2 * i + r + 3)
                            act.wait_ge(weighted, 2 * i + r + 1)
                            nc.scalar.activation(act_sb[:, r], scores[:, r, 0:HALF], ACT.Gelu).then_inc(gelu_done, 1)

                @block.vector
                def _(dve):
                    nc.vector.memset(zero[:], 0.0).then_inc(zeroed, 1)
                    dve.sem_inc(weighted, 2)
                    with dve.Fori(0, P // 2) as i:
                        for r in range(2):
                            dve.wait_ge(gelu_done, 2 * i + r + 3)
                            dve.wait_ge(v_done, 2 * i + r + 1)
                            nc.vector.tensor_tensor(wts[:, r], act_sb[:, r],
                                                    gates[:, ds(2 * i + r, 1)].rearrange("p a n -> p (a n)"),
                                                    ALU.mult).then_inc(weighted, 1)
                    link = Chain(dve, chain_s)
                    dve.wait_ge(v_done, P + 2)
                    for k in range(KT):
                        x = C.X[:, k, t0:t0 + HALF]
                        link(nc.vector.tensor_scalar(wts[:, k % 2], y[:, k], C.m(0, 5, k), None, ALU.mult))
                        nc.vector.scalar_tensor_tensor(out=x, in0=x, scalar=ALPHA, in1=wts[:, k % 2], op0=ALU.mult,
                                                       op1=ALU.add)
    norm_phase(nc, C, "ln2", C.X, C.X, 1, KT, D, EPS_LN, weight=lambda t: C.v("ln2_g", t),
               bias=lambda t: C.v("ln2_b", t), center=True)


def peer_block(nc, io, C):
    with nc.sbuf_tensor("sel", [P, 3, S], F32) as sel:
        peer_select_phase(nc, io, C, sel)
        experts_phase(nc, io, C, sel)



FF_TILES = 22
CHUNK = 64
CHUNKS = S // CHUNK
DECAY = -float(np.exp(-0.5))
SCRATCH = {"cum": (SSD_HEADS, S), "stabilisers": (2, 8, S)}


def swiglu_phases(nc, io, C, layer):
    with nc.sbuf_tensor(f"hid{layer}", [P, FF_TILES, S], F32) as hid:
        with Phase(nc, f"up{layer}") as ph:
            RING = 4
            loaded = [ph.sem(f"loaded{r}") for r in range(RING)]
            projected, silu_done, kept = ph.sem("projected"), ph.sem("silu_done"), ph.sem("kept")
            w = ph.sb("w", [P, RING, KT, P])
            act_sb = ph.sb("act", [P, 2, S])
            acc = ph.ps("acc", [P, RING, S])
            with ph.block() as block:
                @block.sync
                def _(sp):
                    with sp.Fori(0, FF_TILES // 2) as i:
                        for r in range(RING):
                            sp.wait_ge(projected, RING * i + r + 1)
                            sp.dma_start(w[:, r], w_tile(io["w_gu"], i * RING + (2 * FF_TILES * layer + r))
                                         ).then_inc(loaded[r], 16)

                @block.tensor
                def _(pe):
                    pe.sem_inc(projected, RING)
                    with pe.Fori(0, FF_TILES // 2) as i:
                        for r in range(RING):
                            pe.wait_ge(loaded[r], 16 * (i + 1))
                            pe.wait_ge(silu_done if r % 2 == 0 else kept, 2 * i + r // 2 + 1)
                            product(nc, acc[:, r], w[:, r], C.H, KT).then_inc(projected, 1)

                @block.scalar
                def _(act):
                    act.sem_inc(silu_done, 2)
                    with act.Fori(0, FF_TILES // 2) as i:
                        for n in range(2):
                            act.wait_ge(projected, RING * i + 2 * n + 1 + RING)
                            act.wait_ge(kept, 2 * i + n + 1)
                            nc.scalar.activation(act_sb[:, n], acc[:, 2 * n], ACT.Silu).then_inc(silu_done, 1)

                @block.vector
                def _(dve):
                    dve.sem_inc(kept, 2)
                    with dve.Fori(0, FF_TILES // 2) as i:
                        for n in range(2):
                            dve.wait_ge(projected, RING * i + 2 * n + 2 + RING)
                            dve.wait_ge(silu_done, 2 * i + n + 3)
                            nc.vector.tensor_tensor(tile_at(hid, 2 * i + n), act_sb[:, n], acc[:, 2 * n + 1], ALU.mult
                                                    ).then_inc(kept, 1)
        residual_projection(nc, C, f"down{layer}", io["w_down"][KT * layer:KT * layer + KT], hid, FF_TILES,
                            1 + layer, 5, 1.0)


def rwkv_project_phase(nc, io, C, rkv, wl, al, gl, gl2):
    with Phase(nc, "rwproj") as ph:
        loaded = [ph.sem(f"loaded{r}") for r in range(2)]
        small_loaded, mixed, projected, kept, small_done, part_done, diff_s = (ph.sem(n) for n in (
            "small_loaded", "mixed", "projected", "kept", "small_done", "part_done", "diff"))
        w = ph.sb("w", [P, 2, KT, P])
        ws = ph.sb("ws", [P, KT, 288])
        diff = ph.sb("diff", [P, KT, S])
        xs = ph.sb("xs", [P, 2, KT, S])
        acc = ph.ps("acc", [P, 2, S])
        sacc = ph.ps("sacc", [P, 4, S])
        parts = (0, 2, 3, 1, 4, 5)
        with ph.block() as block:
            @block.sync
            def _(sp):
                sp.dma_start(ws[:], io["w_rw_small"]).then_inc(small_loaded, 16)
                with sp.Fori(0, 12) as i:
                    for r in range(2):
                        sp.wait_ge(projected, 2 * i + r + 1)
                        sp.dma_start(w[:, r], w_tile(io["w_rw"], 2 * i + r)).then_inc(loaded[r], 16)

            @block.vector
            def _(dve):
                for k in range(KT):
                    nc.vector.tensor_tensor(diff[:, k, 1:S], C.H[:, k, 0:S - 1], C.H[:, k, 1:S], ALU.subtract)
                    nc.vector.tensor_scalar(diff[:, k, 0:1], C.H[:, k, 0:1], -1.0, None, ALU.mult
                                            ).then_inc(diff_s, 1)
                dve.wait_ge(diff_s, KT)
                for n, which in enumerate(parts):
                    if n >= 2:
                        dve.wait_ge(part_done, n - 1)
                    for k in range(KT):
                        last = nc.vector.scalar_tensor_tensor(out=xs[:, n % 2, k], in0=diff[:, k],
                                                              scalar=C.v("mix", 8 * which + k), in1=C.H[:, k],
                                                              op0=ALU.mult, op1=ALU.add)
                    last.then_inc(mixed, 1)

            @block.tensor
            def _(pe):
                pe.sem_inc(projected, 2)
                for n in range(3):
                    pe.wait_ge(mixed, n + 1)
                    with pe.Fori(4 * n, 4 * n + 4) as i:
                        for r in range(2):
                            pe.wait_ge(loaded[r], 16 * (i + 1))
                            pe.wait_ge(kept, 2 * i + r + 1)
                            product(nc, acc[:, r], w[:, r], xs[:, n % 2], KT).then_inc(projected, 1)
                    pe.wait_ge(projected, 2 + 8 * (n + 1))
                    pe.sem_inc(part_done, 1)
                pe.wait_ge(small_loaded, 16)
                for n, cols in enumerate(((0, 64), (64, 128), (128, 256))):
                    pe.wait_ge(mixed, n + 4)
                    product(nc, sacc[0:cols[1] - cols[0], n], ws[:, :, cols[0]:cols[1]], xs[:, (n + 3) % 2], KT
                            ).then_inc(small_done, 1)
                    if n < 2:
                        pe.wait_ge(small_done, n + 1)
                        pe.sem_inc(part_done, 1)
                product(nc, sacc[0:32, 3], ws[:, :, 256:288], xs[:, 1], KT).then_inc(small_done, 1)

            @block.scalar
            def _(act):
                act.sem_inc(kept, 2)
                with act.Fori(0, 12) as i:
                    for r in range(2):
                        act.wait_ge(projected, 2 * i + r + 3)
                        nc.scalar.activation(tile_at(rkv, 2 * i + r), acc[:, r], ACT.Copy).then_inc(kept, 1)
                act.wait_ge(small_done, 1)
                nc.scalar.activation(wl[:], sacc[0:64, 0], ACT.Tanh)
                act.wait_ge(small_done, 2)
                nc.scalar.activation(al[:], sacc[0:64, 1], ACT.Copy)
                act.wait_ge(small_done, 4)
                nc.scalar.activation(gl[:], sacc[:, 2], ACT.Sigmoid)
                nc.scalar.activation(gl2[:], sacc[0:32, 3], ACT.Sigmoid)


class Rounds:

    def __init__(self, order):
        self.order = [(name, q, who) for name, q, who in order]
        self.index = {(name, q): n for n, (name, q, _) in enumerate(self.order)}
        self.who = {(name, q): w for name, q, w in self.order}
        self.place, counts = {}, {}
        for name, q, w in self.order:
            counts[w] = counts.get(w, 0) + 1
            self.place[name, q] = counts[w]
        self.counts = counts


def rwkv_order():
    steps = [("at", "v"), ("akt", "v"), ("atm", "s"), ("bhm", "s"), ("khm", "s"), ("vtm", "s"), ("x0", "s")]
    order = [(n, q, w) for n, w in steps for q in range(2)]
    for lv in range(1, 6):
        order += [(f"q{lv}", 0, "s"), (f"q{lv}", 1, "s")]
        for q in range(2):
            if lv < 5:
                order.append((f"x{lv}", q, "v"))
            order.append((f"y{lv}", q, "v"))
        if lv == 2:
            order += [("m1", 0, "s"), ("m1", 1, "s")]
    order += [(n, q, w) for n, w in [("p", "s"), ("qm", "s"), ("arb", "v"), ("ark", "v"), ("ft", "v"), ("g", "s"),
                                     ("ht", "v")] for q in range(2)]
    return order


def rwkv_heads_phase(nc, io, C, rkv, wl, al, gl, gl2):
    R = Rounds(rwkv_order())
    NR, NS, NV = len(R.order), R.counts["s"], R.counts["v"]
    BANKS = 5
    with Phase(nc, "rw") as ph:
        names = ("lora_loaded", "lora_done", "front_s", "front_v", "front_p", "rounds", "kept_s", "kept_v", "levels",
                 "chained", "state_kept", "y_ready", "sums", "back_v", "back_s", "pair_done")
        (lora_loaded, lora_done, front_s, front_v, front_p, rounds, kept_s, kept_v, levels, chained, state_kept,
         y_ready, sums, back_v, back_s, pair_done) = (ph.sem(n) for n in names)
        chain_s, chain_p = ph.sem("chain"), ph.sem("pchain")
        w2, a2 = ph.sb("w2", [64, P]), ph.sb("a2", [64, P])
        g2, g2b = ph.sb("g2", [P, P]), ph.sb("g2b", [32, P])
        T = {n: ph.sb(n, [P, S]) for n in ("sgw", "a", "g", "kk0", "sq", "cum", "ce", "dc", "kk", "k2", "ka", "rt",
                                           "bon", "inv")}
        wc = ph.sb("wc", [P, CHUNKS])
        bd = {n: ph.sb(n, [P, CHUNKS, P]) for n in ("at", "bt", "kt", "bh", "kh")}
        vb = ph.sb("vb", [P, CHUNKS, P])
        M = {n: ph.sb("m_" + n, [P, CHUNKS, P]) for n in ("AT", "akt", "lev", "x", "y", "q")}
        M["atm"], M["bhm"], M["khm"], M["vtm"] = (ph.sb("m_" + n, [P, CHUNKS, P]) for n in
                                                  ("atm", "bhm", "khm", "vtm"))
        M["m1"], M["p"], M["qm"] = bd["bh"], M["x"], M["q"]
        M["ft"], M["g"], M["st"] = M["AT"], M["akt"], M["lev"]
        arb, ark, ht = (ph.sb(n, [P, CHUNKS, CHUNK]) for n in ("arb", "ark", "ht"))
        bank = ph.ps("bank", [P, BANKS, 4, P])
        side = ph.ps("side", [P, 3, S])

        def half(buf, q):
            return buf[:, 4 * q:4 * q + 4]

        def blocks(buf, h):
            r = slice(64 * h, 64 * h + 64)
            return buf[r, :, r]

        def of_head(x, h):
            return x[64 * h:64 * h + 64].rearrange("p (c t) -> p c t", t=CHUNK)

        with ph.block() as block:
            @block.sync
            def _(sp):
                with sp.Fori(0, KT) as i:
                    sp.wait_ge(lora_done, 3 * i)
                    for dst, src in ((w2, io["w2"][ds(i, 1)]), (a2, io["a2"][ds(i, 1)]),
                                     (g2, io["g2"][ds(i, 1), 0:P]), (g2b, io["g2"][ds(i, 1), P:160])):
                        sp.dma_start(dst[:], src.rearrange("a p n -> (a p) n")).then_inc(lora_loaded, 16)

            @block.tensor
            def _(pe):
                with pe.Fori(0, KT) as i:
                    pe.wait_ge(lora_loaded, 64 * (i + 1))
                    pe.wait_ge(pair_done, i + 0)
                    nc.tensor.matmul(side[:, 0], w2[:], wl[:], start=True, stop=True).then_inc(lora_done, 1)
                    nc.tensor.matmul(side[:, 1], a2[:], al[:], start=True, stop=True).then_inc(lora_done, 1)
                    nc.tensor.matmul(side[:, 2], g2[:], gl[:], start=True, stop=False)
                    nc.tensor.matmul(side[:, 2], g2b[:], gl2[:], start=False, stop=True).then_inc(lora_done, 1)
                    pe.wait_ge(front_s, 12 * i + 4)
                    nc.tensor.matmul(side[:, 0], C.ones_bd[:], T["sq"][:], start=True, stop=True).then_inc(sums, 1)
                    pe.wait_ge(front_v, 8 * i + 8)
                    pe.wait_ge(front_s, 12 * i + 12)
                    nc.tensor.matmul(side[:, 1], C.ones_bd[:], T["sq"][:], start=True, stop=True).then_inc(sums, 1)

                    def need(*results):
                        for sem, per, who in ((kept_s, NS, "s"), (kept_v, NV, "v")):
                            places = [R.place[x] for x in results if R.who[x] == who]
                            if places:
                                pe.wait_ge(sem, per * i + max(places))

                    def free(n):
                        return [R.order[n - BANKS][:2]] if n >= BANKS else []

                    def round_(name, q, products, *needs, width=P):
                        n = R.index[name, q]
                        need(*free(n), *needs)
                        for j in range(4):
                            ops = products(4 * q + j)
                            for k, (a, b) in enumerate(ops):
                                last = nc.tensor.matmul(bank[:, n % BANKS, j, 0:width], a, b, start=(k == 0),
                                                        stop=(k == len(ops) - 1))
                        last.then_inc(rounds, 1)

                    def turn(name, q, src):
                        n = R.index[name, q]
                        need(*free(n))
                        for j in range(4):
                            last = nc.tensor.transpose(bank[:, n % BANKS, j], src[:, 4 * q + j], C.ident[:])
                        last.then_inc(rounds, 1)

                    for q in range(2):
                        round_("at", q, lambda c: [(bd["bt"][:, c], bd["at"][:, c])])
                    for q in range(2):
                        round_("akt", q, lambda c: [(bd["kt"][:, c], bd["at"][:, c])])
                    for name, src in (("atm", bd["at"]), ("bhm", bd["bh"]), ("khm", bd["kh"]), ("vtm", vb)):
                        for q in range(2):
                            turn(name, q, src)
                    for q in range(2):
                        pe.wait_ge(levels, 12 * i + 1 + q)
                        turn("x0", q, M["y"])
                    for lv in range(1, 6):
                        for q in range(2):
                            pe.wait_ge(levels, 12 * i + 2 * lv + 1 + q)
                            round_(f"q{lv}", q, lambda c: [(M["lev"][:, c], M["x"][:, c])], (f"x{lv - 1}", q))
                        for q in range(2):
                            y_kept = [(f"y{lv - 1}", q)] if lv > 1 else []
                            if lv < 5:
                                round_(f"x{lv}", q, lambda c: [(M["y"][:, c], M["q"][:, c])], (f"q{lv}", q), *y_kept)
                            round_(f"y{lv}", q, lambda c: [(M["q"][:, c], M["y"][:, c])], (f"q{lv}", q), *y_kept)
                        if lv == 2:
                            for q in range(2):
                                round_("m1", q, lambda c: [(M["akt"][:, c], M["vtm"][:, c])], ("akt", q), ("vtm", q))
                    for q in range(2):
                        round_("p", q, lambda c: [(M["y"][:, c], M["atm"][:, c])], ("y5", q), ("atm", q))
                    for q in range(2):
                        round_("qm", q, lambda c: [(M["y"][:, c], M["m1"][:, c])], ("m1", q))
                    for name, lhs in (("arb", bd["bt"]), ("ark", bd["kt"])):
                        for q in range(2):
                            round_(name, q, lambda c: [(lhs[:, c], T["rt"][:, c * CHUNK:(c + 1) * CHUNK])],
                                   width=CHUNK)
                    for q in range(2):
                        round_("ft", q, lambda c: [(M["p"][:, c], M["bhm"][:, c])], ("p", q), ("bhm", q))
                    for q in range(2):
                        round_("g", q, lambda c: [(M["bhm"][:, c], M["qm"][:, c]), (M["khm"][:, c], M["vtm"][:, c])],
                               ("qm", q), ("khm", q))
                    for q in range(2):
                        round_("ht", q, lambda c: [(M["p"][:, c], arb[:, c])], ("arb", q), width=CHUNK)
                    need(("g", 1), ("ht", 1))
                    for c in range(1, CHUNKS):
                        pe.wait_ge(state_kept, 7 * i + c)
                        if c < CHUNKS - 1:
                            nc.tensor.matmul(bank[:, c % 2, 0], M["ft"][:, c], M["st"][:, c], start=True, stop=True
                                             ).then_inc(chained, 1)
                    for c in range(CHUNKS):
                        out = side[:, 2, c * CHUNK:(c + 1) * CHUNK]
                        ops = [(M["qm"][:, c], arb[:, c]), (M["vtm"][:, c], ark[:, c])]
                        if c:
                            ops.append((M["st"][:, c], ht[:, c]))
                        for k, (a, b) in enumerate(ops):
                            last = nc.tensor.matmul(out, a, b, start=(k == 0), stop=(k == len(ops) - 1))
                    last.then_inc(y_ready, 1)
                    pe.wait_ge(back_v, 3 * i + 1)
                    nc.tensor.matmul(side[:, 0], C.ones_bd[:], T["cum"][:], start=True, stop=True).then_inc(sums, 1)
                    pe.wait_ge(back_s, 2 * i + 1)
                    nc.tensor.matmul(side[:, 0], C.ones_bd[:], T["sq"][:], start=True, stop=True).then_inc(sums, 1)

            @block.scalar
            def _(act):
                with act.Fori(0, KT) as i:
                    def front(ins):
                        ins.then_inc(front_s, 1)
                    act.wait_ge(lora_done, 3 * i + 3)
                    front(nc.scalar.activation(T["sgw"][:], side[:, 0], ACT.Sigmoid, bias=C.v("w0", i)))
                    front(nc.scalar.activation(T["a"][:], side[:, 1], ACT.Sigmoid, bias=C.v("a0", i)))
                    front(nc.scalar.activation(T["g"][:], side[:, 2], ACT.Copy))
                    act.wait_ge(front_v, 8 * i + 1)
                    front(nc.scalar.activation(T["sq"][:], T["kk0"][:], ACT.Square))
                    act.wait_ge(sums, 4 * i + 1)
                    front(nc.scalar.activation(T["inv"][:], side[:, 0], ACT.Sqrt))
                    v = rkv[:, ds(i + 16, 1)].rearrange("p a n -> p (a n)")
                    for h in range(2):
                        front(nc.scalar.activation(blocks(vb, h), of_head(v, h), ACT.Copy))
                    act.wait_ge(front_v, 8 * i + 2)
                    last = T["cum"][:].rearrange("p (c t) -> p c t", t=CHUNK)[:, :, CHUNK - 1]
                    front(nc.scalar.activation(wc[:], last, ACT.Exp))
                    front(nc.scalar.activation(T["ce"][:], T["ce"][:], ACT.Exp))
                    front(nc.scalar.activation(T["dc"][:], T["dc"][:], ACT.Exp))
                    front(nc.scalar.activation(T["sgw"][:], T["cum"][:], ACT.Exp, scale=-1.0))
                    act.wait_ge(front_s, 12 * i + 11)
                    front(nc.scalar.activation(T["cum"][:], T["cum"][:], ACT.Exp))

                    def keep(name, q, dst):
                        n = R.index[name, q]
                        act.wait_ge(rounds, NR * i + n + 1)
                        nc.scalar.activation(half(dst, q), bank[:, n % BANKS], ACT.Copy).then_inc(kept_s, 1)
                    for name in ("atm", "bhm", "khm", "vtm"):
                        for q in range(2):
                            keep(name, q, M[name])
                    for q in range(2):
                        keep("x0", q, M["x"])
                    for lv in range(1, 6):
                        for q in range(2):
                            keep(f"q{lv}", q, M["q"])
                        if lv == 2:
                            for q in range(2):
                                keep("m1", q, M["m1"])
                    for q in range(2):
                        keep("p", q, M["p"])
                    for q in range(2):
                        keep("qm", q, M["qm"])
                    for q in range(2):
                        keep("g", q, M["g"])
                    act.wait_ge(back_v, 3 * i + 2)
                    nc.scalar.activation(T["sq"][:], T["cum"][:], ACT.Square).then_inc(back_s, 1)
                    act.wait_ge(back_v, 3 * i + 3)
                    nc.scalar.activation(T["inv"][:], T["inv"][:], ACT.Sqrt).then_inc(back_s, 1)

            @block.gpsimd
            def _(pool):
                for n, buf in enumerate([*bd.values(), vb]):
                    nc.gpsimd.memset(buf[:].rearrange("p a n -> p (a n)"), 0.0).then_inc(front_p, 1)

            @block.vector
            def _(dve):
                link = Chain(dve, chain_s)
                tt = nc.vector.tensor_tensor
                dve.wait_ge(front_p, 6)
                with dve.Fori(0, KT) as i:
                    link.restart()
                    r, k, v = (rkv[:, ds(i + n, 1)].rearrange("p a n -> p (a n)") for n in (0, 8, 16))
                    nc.vector.tensor_scalar(T["kk0"][:], k, C.v("k_k", i), None, ALU.mult).then_inc(front_v, 1)
                    dve.wait_ge(front_s, 12 * i + 3)
                    link(nc.vector.tensor_scalar(T["sgw"][:], T["sgw"][:], DECAY, None, ALU.mult))
                    link(nc.vector.tensor_tensor_scan(T["cum"][:], C.carry[:], T["sgw"][:], 0.0, ALU.mult, ALU.add))
                    link(tt(T["ce"][:], T["cum"][:], T["sgw"][:], ALU.subtract))
                    cum = T["cum"][:].rearrange("p (c t) -> p c t", t=CHUNK)
                    tt(T["dc"][:].rearrange("p (c t) -> p c t", t=CHUNK),
                       cum[:, :, CHUNK - 1:CHUNK].broadcast_to([P, CHUNKS, CHUNK]), cum, ALU.subtract
                       ).then_inc(front_v, 1)
                    dve.wait_ge(front_s, 12 * i + 5)
                    link(nc.vector.tensor_scalar(T["inv"][:], T["inv"][:], 1e-12, None, ALU.max))
                    link(nc.vector.reciprocal(T["inv"][:], T["inv"][:]))
                    link(tt(T["kk"][:], T["kk0"][:], T["inv"][:], ALU.mult))
                    link(nc.vector.tensor_scalar(T["k2"][:], T["a"][:], -1.0, C.v("k_a", i), ALU.add, ALU.mult))
                    link(nc.vector.scalar_tensor_tensor(out=T["k2"][:], in0=T["k2"][:], scalar=1.0, in1=k,
                                                        op0=ALU.add, op1=ALU.mult))
                    link(tt(T["ka"][:], T["kk"][:], T["a"][:], ALU.mult))
                    dve.wait_ge(front_s, 12 * i + 12)
                    for n, (name, x, e) in enumerate((("at", "kk", "ce"), ("bt", "ka", "sgw"), ("kt", "k2", "sgw"),
                                                      ("bh", "ka", "dc"), ("kh", "k2", "dc"))):
                        for h in range(2):
                            last = nc.vector.scalar_tensor_tensor(
                                out=blocks(bd[name], h), in0=of_head(T[x], h), scalar=(-1.0 if name == "at" else 1.0),
                                in1=of_head(T[e], h), op0=ALU.mult, op1=ALU.mult)
                        last.then_inc(front_v, 1)
                    dve.wait_ge(front_s, 12 * i + 12)
                    link(tt(T["rt"][:], r, T["cum"][:], ALU.mult))
                    nc.vector.scalar_tensor_tensor(out=T["sq"][:], in0=r, scalar=C.v("r_k", i), in1=T["k2"][:],
                                                   op0=ALU.mult, op1=ALU.mult).then_inc(front_v, 1)

                    def of(name, q):
                        return bank[:, R.index[name, q] % BANKS]

                    def read(name, q):
                        dve.wait_ge(rounds, NR * i + R.index[name, q] + 1)
                        return of(name, q)

                    def kept(ins, name, q):
                        ins.then_inc(kept_v, 1)
                        dve.wait_ge(kept_v, NV * i + R.place[name, q])

                    def wide(m):
                        return m.unsqueeze(1).broadcast_to([P, 4, P])

                    for q in range(2):
                        kept(tt(half(M["AT"], q), read("at", q), wide(C.strict[:]), ALU.mult), "at", q)
                    for q in range(2):
                        link(tt(half(M["y"], q), half(M["AT"], q), wide(C.level[:, 0]), ALU.mult))
                        tt(half(M["y"], q), half(M["y"], q), wide(C.ident[:]), ALU.add).then_inc(levels, 1)
                    for q in range(2):
                        kept(tt(half(M["akt"], q), read("akt", q), wide(C.strict[:]), ALU.mult), "akt", q)
                    for lv in range(1, 6):
                        for q in range(2):
                            if lv > 1:
                                dve.wait_ge(rounds, NR * i + R.index[f"q{lv - 1}", q] + 1)
                            tt(half(M["lev"], q), half(M["AT"], q), wide(C.level[:, lv]), ALU.mult
                               ).then_inc(levels, 1)
                        for q in range(2):
                            dve.wait_ge(rounds, NR * i + R.index[f"y{lv}", q] + 1)
                            if lv < 5:
                                kept(tt(half(M["x"], q), half(M["x"], q), of(f"x{lv}", q), ALU.add), f"x{lv}", q)
                            kept(tt(half(M["y"], q), half(M["y"], q), of(f"y{lv}", q), ALU.add), f"y{lv}", q)
                    for name, dst in (("arb", arb), ("ark", ark)):
                        for q in range(2):
                            kept(tt(half(dst, q), read(name, q)[:, :, 0:CHUNK],
                                    C.keep64[:].unsqueeze(1).broadcast_to([P, 4, CHUNK]), ALU.mult), name, q)
                    for q in range(2):
                        src = read("ft", q)
                        for j in range(4):
                            c = 4 * q + j
                            ins = nc.vector.scalar_tensor_tensor(out=M["ft"][:, c], in0=C.ident[:],
                                                                 scalar=wc[:, c:c + 1], in1=src[:, j],
                                                                 op0=ALU.mult, op1=ALU.add)
                        kept(ins, "ft", q)
                    rt = T["rt"][:].rearrange("p (c t) -> p c t", t=CHUNK)
                    for q in range(2):
                        kept(tt(half(ht, q), read("ht", q)[:, :, 0:CHUNK], half(rt, q), ALU.add), "ht", q)
                    dve.wait_ge(kept_s, NS * i + R.place["g", 1])
                    nc.vector.tensor_copy(M["st"][:, 1], M["g"][:, 0]).then_inc(state_kept, 1)
                    for c in range(1, CHUNKS - 1):
                        dve.wait_ge(chained, 6 * i + c)
                        tt(M["st"][:, c + 1], M["g"][:, c], bank[:, c % 2, 0], ALU.add).then_inc(state_kept, 1)
                    dve.wait_ge(sums, 4 * i + 2)
                    link(tt(T["bon"][:], v, side[:, 1], ALU.mult))
                    dve.wait_ge(y_ready, i + 1)
                    nc.vector.tensor_copy(T["cum"][:], side[:, 2]).then_inc(back_v, 1)
                    dve.wait_ge(back_v, 3 * i + 1)
                    dve.wait_ge(sums, 4 * i + 3)
                    nc.vector.scalar_tensor_tensor(out=T["cum"][:], in0=side[:, 0], scalar=-1.0 / CHUNK, in1=T["cum"][:],
                                                   op0=ALU.mult, op1=ALU.add).then_inc(back_v, 1)
                    dve.wait_ge(back_v, 3 * i + 2)
                    dve.wait_ge(sums, 4 * i + 4)
                    nc.vector.tensor_scalar(T["inv"][:], side[:, 0], 1.0 / CHUNK, EPS_GN, ALU.mult, ALU.add
                                            ).then_inc(back_v, 1)
                    dve.wait_ge(back_s, 2 * i + 2)
                    link(nc.vector.reciprocal(T["inv"][:], T["inv"][:]))
                    link(nc.vector.scalar_tensor_tensor(out=T["cum"][:], in0=T["cum"][:], scalar=C.v("gn_w", i),
                                                        in1=T["inv"][:], op0=ALU.mult, op1=ALU.mult))
                    link(nc.vector.scalar_tensor_tensor(out=T["cum"][:], in0=T["cum"][:], scalar=C.v("gn_b", i),
                                                        in1=T["bon"][:], op0=ALU.add, op1=ALU.add))
                    link(tt(r, T["cum"][:], T["g"][:], ALU.mult))
                    dve.sem_inc(pair_done, 1)


def mlstm_gates_phase(nc, io, C, ngc):
    with Phase(nc, "mlgates") as ph:
        names = ("loaded", "projected", "bias_ready", "capped", "front", "logged", "rows_ready", "em", "turned", "stored")
        loaded, projected, bias_ready, capped, front, logged, rows_ready, em_s, turned, stored = (
            ph.sem(n) for n in names)
        chain_s = ph.sem("chain")
        w = ph.sb("w", [P, KT, 16])
        b = ph.sb("b", [8, 2])
        li, fx, t, f, ng, m, one, em = (ph.sb(n, [8, S]) for n in ("li", "fx", "t", "f", "ng", "m", "one", "em"))
        acc = ph.ps("acc", [P, 2, S])
        tps = ph.ps("tps", [P, TB, 8])
        with ph.block() as block:
            @block.sync
            def _(sp):
                sp.dma_start(w[:], io["w_ml_gates"]).then_inc(loaded, 16)
                sp.wait_ge(rows_ready, 2)
                sp.dma_start(io["stabilisers"][0], m[:]).then_inc(stored, 16)
                sp.wait_ge(em_s, 1)
                sp.dma_start(io["stabilisers"][1], em[:]).then_inc(stored, 16)
                sp.wait_ge(stored, 32)

            @block.tensor
            def _(pe):
                pe.wait_ge(loaded, 16)
                for n in range(2):
                    product(nc, acc[0:8, n], w[:, :, 8 * n:8 * n + 8], C.H, KT).then_inc(projected, 1)
                pe.wait_ge(rows_ready, 1)
                for tb in range(TB):
                    last = nc.tensor.transpose(tps[:, tb], ng[:, tb * P:(tb + 1) * P], C.ident[0:8, 0:8])
                last.then_inc(turned, 1)

            @block.scalar
            def _(act):
                act.wait_ge(bias_ready, 1)
                act.wait_ge(projected, 2)
                for n, dst in enumerate((li, fx)):
                    nc.scalar.activation(dst[:], acc[0:8, n], ACT.Tanh, bias=b[:, n:n + 1], scale=1.0 / 15.0
                                         ).then_inc(capped, 1)
                act.wait_ge(front, 1)
                nc.scalar.activation(t[:], t[:], ACT.Exp, scale=-1.0).then_inc(logged, 1)
                act.wait_ge(front, 2)
                nc.scalar.activation(t[:], t[:], ACT.Ln).then_inc(logged, 1)
                act.wait_ge(front, 3)
                nc.scalar.activation(em[:], em[:], ACT.Exp, scale=-1.0).then_inc(em_s, 1)
                act.wait_ge(turned, 1)
                nc.scalar.activation(ngc[:], tps[:], ACT.Copy)

            @block.vector
            def _(dve):
                link = Chain(dve, chain_s)
                link(nc.vector.memset(one[:], 1.0))
                nc.vector.tensor_scalar(b[:], C.v("head_ml", 0, 2)[0:8], 1.0 / 15.0, None, ALU.mult
                                        ).then_inc(bias_ready, 1)
                dve.wait_ge(capped, 2)
                link(nc.vector.tensor_scalar(li[:], li[:], 15.0, None, ALU.mult))
                link(nc.vector.tensor_scalar(fx[:], fx[:], 15.0, None, ALU.mult))
                nc.vector.scalar_tensor_tensor(out=t[:], in0=fx[:], scalar=-1.0, in1=fx[:], op0=ALU.mult, op1=ALU.max
                                               ).then_inc(front, 1)
                dve.wait_ge(logged, 1)
                nc.vector.tensor_scalar(t[:], t[:], 1.0, None, ALU.add).then_inc(front, 1)
                dve.wait_ge(logged, 2)
                link(nc.vector.scalar_tensor_tensor(out=fx[:], in0=fx[:], scalar=0.0, in1=t[:], op0=ALU.min,
                                                    op1=ALU.subtract))
                link(nc.vector.tensor_tensor_scan(f[:], one[:], fx[:], 0.0, ALU.mult, ALU.add))
                nc.vector.tensor_tensor(ng[:], f[:], li[:], ALU.subtract).then_inc(rows_ready, 1)
                dve.wait_ge(rows_ready, 1)
                nc.vector.tensor_tensor_scan(m[:], ng[:], ng[:], 0.0, ALU.min, ALU.min).then_inc(rows_ready, 1)
                dve.wait_ge(rows_ready, 2)
                nc.vector.tensor_tensor(em[:], f[:], m[:], ALU.subtract).then_inc(front, 1)


def mlstm_phase(nc, io, C, out, gate, ngc):
    with Phase(nc, "ml") as ph:
        loaded = [ph.sem(f"loaded{n}") for n in range(6)]
        names = ("rows_loaded", "projected", "u_kept", "qk_ready", "conv_done", "v_kept", "gate_kept", "cb_ready",
                 "cb_kept", "shifted", "exp_done", "weighted", "summed", "den_kept", "head_done")
        (rows_loaded, projected, u_kept, qk_ready, conv_done, v_kept, gate_kept, cb_ready, cb_kept, shifted, exp_done,
         weighted, summed, den_kept, head_done) = (ph.sem(n) for n in names)
        chain_s = ph.sem("chain")
        w = ph.sb("w", [P, 6, KT, P])
        rows = ph.sb("rows", [P, 4, S])
        u = ph.sb("u", [P, 2, S + 3])
        pre = ph.sb("pre", [P, 2, S])
        qk = ph.sb("qk", [P, 2, S])
        v = ph.sb("v", [P, 2, TB, P])
        cb, e = ph.sb("cb", [P, 2, CB_LEN]), ph.sb("e", [P, 2, CB_LEN])
        den, inv = ph.sb("den", [P, S]), ph.sb("inv", [P, S])
        proj = ph.ps("proj", [P, 3, S])
        cps = ph.ps("cps", [P, 2, S])
        nps = ph.ps("nps", [P, 2, S])
        PAIRS = 4
        with ph.block() as block:
            @block.sync
            def _(sp):
                with sp.Fori(0, PAIRS) as i:
                    for n, tile in enumerate((i, i + 4, 2 * i + 16, 2 * i + 17, 2 * i + 8, 2 * i + 9)):
                        sp.wait_ge(projected, 6 * i + n + 1)
                        sp.dma_start(w[:, n], w_tile(io["w_ml"], tile)).then_inc(loaded[n], 16)
                    sp.wait_ge(head_done, 2 * i)
                    for h in range(2):
                        for n in range(2):
                            sp.dma_start(rows[:, 2 * h + n], io["stabilisers"][n, ds(2 * i + h, 1)].broadcast_to([P, S])
                                         ).then_inc(rows_loaded, 16)

            @block.tensor
            def _(pe):
                pe.sem_inc(projected, 6)

                def bank_free(i, n):
                    if n in (0, 1):
                        pe.wait_ge(v_kept if n else gate_kept, 2 * i + (1 if n else 2) - 0)
                    elif n == 2:
                        pe.wait_ge(v_kept, 2 * i + 2)
                    elif n in (3, 4):
                        pe.wait_ge(u_kept, 2 * i + n - 2)
                    else:
                        pe.wait_ge(gate_kept, 2 * i + 3)

                def project(i):
                    for n in range(4):
                        pe.wait_ge(loaded[n], 16 * (i + 1))
                        bank_free(i, n)
                        product(nc, proj[:, n % 3], w[:, n], C.H, KT).then_inc(projected, 1)
                    for n in (4, 5):
                        pe.wait_ge(loaded[n], 16 * (i + 1))
                        bank_free(i, n)
                        for tb in range(TB):
                            for k in range(KT):
                                last = nc.tensor.matmul(proj[:, n % 3, tb * P:(tb + 1) * P],
                                                        C.H[:, k, tb * P:(tb + 1) * P], w[:, n, k],
                                                        start=(k == 0), stop=(k == KT - 1))
                        last.then_inc(projected, 1)

                with pe.Fori(0, PAIRS) as i:
                    project(i)
                    pe.wait_ge(qk_ready, 2 * i + 2)
                    for h in range(2):
                        r = slice(64 * h, 64 * h + 64)
                        for sb in range(TB):
                            n = 4 * h + sb
                            pe.wait_ge(cb_kept, 8 * i + n + 1)
                            nc.tensor.matmul(cps[:, n % 2, 0:S - sb * P], qk[r, 1, sb * P:(sb + 1) * P],
                                             qk[r, 0, sb * P:S], start=True, stop=True).then_inc(cb_ready, 1)
                    pe.wait_ge(v_kept, 2 * i + 4)
                    for h in range(2):
                        pe.wait_ge(weighted, 2 * i + h + 1)
                        pe.wait_ge(head_done, 2 * i + h)
                        for n in range(2):
                            for sb in range(TB):
                                last = nc.tensor.matmul(nps[:, n, sb * P:S], C.ones[:] if n else v[:, h, sb],
                                                        e[:, h, cb_slice(sb)], start=(sb == 0), stop=(sb == TB - 1))
                        last.then_inc(summed, 1)

            @block.scalar
            def _(act):
                act.sem_inc(gate_kept, 2)
                act.sem_inc(v_kept, 2)
                with act.Fori(0, PAIRS) as i:
                    for n in range(2):
                        act.wait_ge(projected, 6 * i + n + 7)
                        act.wait_ge(conv_done, 2 * i + n + 1)
                        nc.scalar.activation(u[:, n, 3:], proj[:, n], ACT.Copy).then_inc(u_kept, 1)
                    for n in range(2):
                        act.wait_ge(projected, 6 * i + n + 9)
                        nc.scalar.activation(tile_at(gate, 2 * i + n), proj[:, (n + 2) % 3], ACT.Sigmoid
                                             ).then_inc(gate_kept, 1)
                    for n in range(2):
                        act.wait_ge(projected, 6 * i + n + 11)
                        act.wait_ge(head_done, 2 * i)
                        nc.scalar.activation(v[:, n].rearrange("p a n -> p (a n)"), proj[:, (n + 4) % 3], ACT.Copy
                                             ).then_inc(v_kept, 1)
                    for n in range(2):
                        act.wait_ge(conv_done, 2 * i + n + 3)
                        nc.scalar.activation(qk[:, n], pre[:, n], ACT.Silu).then_inc(qk_ready, 1)
                    for h in range(2):
                        act.wait_ge(shifted, 2 * i + h + 1)
                        nc.scalar.activation(e[:, h], e[:, h], ACT.Exp).then_inc(exp_done, 1)
                    for h in range(2):
                        act.wait_ge(summed, 2 * i + h + 1)
                        act.wait_ge(head_done, 2 * i + h)
                        nc.scalar.activation(den[:], nps[:, 1], ACT.Copy).then_inc(den_kept, 1)

            @block.vector
            def _(dve):
                link = Chain(dve, chain_s)
                for n in range(2):
                    nc.vector.memset(u[:, n, 0:3], 0.0).then_inc(conv_done, 1)
                dve.sem_inc(cb_kept, 2)
                with dve.Fori(0, PAIRS) as i:
                    link.restart()
                    for n in range(2):
                        dve.wait_ge(u_kept, 2 * i + n + 1)
                        conv_silu_front(nc, dve, link, u[:, n], pre[:, n], lambda j, c: C.v(f"ml_w{j}", c),
                                        lambda c: C.v("ml_cb", c), i + 4 * n).then_inc(conv_done, 1)
                    dve.wait_ge(rows_loaded, 64 * (i + 1))
                    for h in range(2):
                        decay_weights(nc, dve, e[:, h], rows[:, 2 * h],
                                      lambda sb: ngc[:, sb, ds(2 * i + h, 1)]).then_inc(shifted, 1)
                    for h in range(2):
                        for sb in range(TB):
                            n = 4 * h + sb
                            dve.wait_ge(cb_ready, 8 * i + n + 1)
                            at = CB_AT[sb]
                            if sb < TB - 1:
                                nc.vector.tensor_copy(cb[:, h, at + P:at + S - sb * P], cps[:, n % 2, P:S - sb * P])
                            nc.vector.tensor_tensor(cb[:, h, at:at + P], cps[:, n % 2, 0:P], C.keep[:], ALU.mult
                                                    ).then_inc(cb_kept, 1)
                    dve.wait_ge(cb_kept, 8 * i + 10)
                    for h in range(2):
                        dve.wait_ge(exp_done, 2 * i + h + 1)
                        nc.vector.scalar_tensor_tensor(out=e[:, h], in0=e[:, h], scalar=0.125, in1=cb[:, h],
                                                       op0=ALU.mult, op1=ALU.mult).then_inc(weighted, 1)
                    for h in range(2):
                        dve.wait_ge(den_kept, 2 * i + h + 1)
                        link(nc.vector.scalar_tensor_tensor(out=inv[:], in0=den[:], scalar=-1.0, in1=den[:],
                                                            op0=ALU.mult, op1=ALU.max))
                        link(nc.vector.tensor_tensor(inv[:], inv[:], rows[:, 2 * h + 1], ALU.max))
                        link(nc.vector.reciprocal(inv[:], inv[:]))
                        nc.vector.tensor_tensor(tile_at(out, 2 * i + h), nps[:, 0], inv[:], ALU.mult
                                                ).then_inc(head_done, 1)


def second_block(nc, io, C):
    rms = dict(groups=1, size=KT, count=D, eps=EPS_RMS)
    norm_phase(nc, C, "rms0", C.X, C.H, mod=(1, 0), **rms)
    with ExitStack() as ctx:
        def sb(name, shape):
            return ctx.enter_context(nc.sbuf_tensor(name, shape, F32))
        rkv = sb("rkv", [P, 24, S])
        wl, al, gl, gl2 = sb("wl", [64, S]), sb("al", [64, S]), sb("gl", [P, S]), sb("gl2", [32, S])
        rwkv_project_phase(nc, io, C, rkv, wl, al, gl, gl2)
        rwkv_heads_phase(nc, io, C, rkv, wl, al, gl, gl2)
        residual_projection(nc, C, "rwout", io["w_rw_out"], rkv, KT, 1, 2, 1.0)
    norm_phase(nc, C, "rms1", C.X, C.H, mod=(1, 3), **rms)
    swiglu_phases(nc, io, C, 0)
    norm_phase(nc, C, "rms2", C.X, C.H, mod=(2, 0), **rms)
    with ExitStack() as ctx:
        def sb(name, shape):
            return ctx.enter_context(nc.sbuf_tensor(name, shape, F32))
        h, gate = sb("ml_h", [P, KT, S]), sb("ml_gate", [P, KT, S])
        ngc = sb("ngc", [P, TB, 8])
        mlstm_gates_phase(nc, io, C, ngc)
        mlstm_phase(nc, io, C, h, gate, ngc)
        norm_phase(nc, C, "mlnorm", h, h, KT, 1, P, EPS_RMS, weight=lambda t: C.v("hn_w", t), times=gate)
        residual_projection(nc, C, "mlout", io["w_ml_out"], h, KT, 2, 2, 1.0)
    norm_phase(nc, C, "rms3", C.X, C.H, mod=(2, 3), **rms)
    swiglu_phases(nc, io, C, 1)
    norm_phase(nc, C, "rmsf", C.X, C.H, weight=lambda t: C.v("final", t), **rms)



class Consts:

    def __init__(self, nc, ctx):
        def sb(name, shape, dt=F32):
            return ctx.enter_context(nc.sbuf_tensor(name, shape, dt))
        self.X, self.H = sb("X", [P, KT, S]), sb("H", [P, KT, S])
        self.vec = sb("vec", [P, VEC_COLS])
        self.mod = sb("mod", [P, 144])
        self.csil = sb("csil", [P, 16])
        self.ones, self.ones_bd, self.ident = sb("ones", [P, P]), sb("ones_bd", [P, P]), sb("ident", [P, P])
        self.keep, self.keep64, self.strict = sb("keep", [P, P]), sb("keep64", [P, 64]), sb("strict", [P, P])
        self.level = sb("level", [P, 6, P])
        self.dist, self.carry = sb("dist", [P, S]), sb("carry", [P, S])
        self.iota = sb("iota", [P, P])
        self.nslope, self.nlam, self.subln = sb("nslope", [P, 8]), sb("nlam", [P, 1]), sb("subln", [P, 1])

    def v(self, name, k=0, n=1):
        return self.vec[:, ds(VEC_AT[name] + k, n)]

    def m(self, layer, part, k):
        col = 48 * layer + 8 * part + k
        return self.mod[:, col:col + 1]


def build(nc, io):
    with ExitStack() as ctx:
        C = Consts(nc, ctx)

        first_block(nc, io, C)
        second_block(nc, io, C)
        with Phase(nc, "store") as ph:
            stored = ph.sem("stored")
            with ph.block() as block:
                @block.sync
                def _(sp):
                    sp.dma_start(io["out"], C.H[:]).then_inc(stored, 16)
                    sp.wait_ge(stored, 16)



def tiles(w, n=P):
    rows, cols = w.shape
    return np.ascontiguousarray(w.reshape(rows // P, P, cols // n, n).transpose(2, 1, 0, 3))


def columns(v):
    return np.asarray(v).reshape(-1, P).T


def layouts(i):
    i = {k: np.asarray(v) for k, v in i.items()}
    w_in = i["w_in"][0]
    o_dt = 8192
    arrays = {
        "x": i["x"][0].T.reshape(KT, P, S).transpose(1, 0, 2),
        "w_ada": np.concatenate([tiles(w, 512) for w in (i["w_ada"][0], i["ada_w_2"][0], i["ada_w_2"][1])]),
        "w_in": tiles(np.concatenate([w_in[:, :o_dt], w_in[:, o_dt + 32:]], axis=1)),
        "w_dt": w_in[:, o_dt:o_dt + 32].reshape(KT, P, 32).transpose(1, 0, 2),
        "w_attn_branch": tiles(i["w_attn_branch"][0]),
        "w_ssd_branch": tiles(i["w_ssd_branch"][0]),
        "w_out": tiles(i["w_out"][0]),
        "w_query": tiles(i["peer_w_query"][0]),
        "keys": i["peer_sub_keys"][0].transpose(2, 0, 1),
        "u": i["peer_u"][0].reshape(P, P, KT, P).transpose(0, 3, 2, 1),
        "v": i["peer_v"][0].reshape(P, P, D),
    }
    def pad(v):
        v = np.asarray(v).reshape(-1)
        return np.concatenate([v, np.zeros(P - v.size, v.dtype)])[:, None]
    conv, mlc = i["conv_w"][0], i["ml_conv_w_2"][0]
    parts = {
        "c": columns(i["c"]), "c2": columns(i["c_2"]), "b_ada": columns(i["b_ada"]), "ada_b2": columns(i["ada_b_2"]),
        **{f"conv_w{n}": columns(conv[n]) for n in range(4)}, "conv_b": columns(i["conv_b"]),
        "d_skip": columns(np.repeat(i["d_skip"][0], 64)), "ssd_norm": columns(i["ssd_norm_w"]),
        "subln": columns(i["da_subln_w"]),
        "lam": np.concatenate([pad(i[f"lambda_{n}"]) for n in ("q1", "k1", "q2", "k2")], axis=1),
        "head_ssd": np.concatenate([pad(i["dt_bias"]), pad(i["a_log"])], axis=1),
        "head_ml": np.concatenate([pad(i["ml_b_i_2"]), pad(i["ml_b_f_2"])], axis=1),
        "ln1_g": columns(i["ln1_g"]), "ln1_b": columns(i["ln1_b"]),
        "ln2_g": columns(i["ln2_g"]), "ln2_b": columns(i["ln2_b"]),
        "mix": columns(i["rw_mix_2"]), "w0": columns(i["rw_w0_2"]), "a0": columns(i["rw_a0_2"]),
        "k_k": columns(i["rw_k_k_2"]), "k_a": columns(i["rw_k_a_2"]), "r_k": columns(i["rw_r_k_2"]),
        "gn_w": columns(i["rw_gn_w_2"]), "gn_b": columns(i["rw_gn_b_2"]),
        **{f"ml_w{n}": columns(mlc[n]) for n in range(4)}, "ml_cb": columns(i["ml_conv_b_2"]),
        "hn_w": columns(i["ml_hn_w_2"]), "final": columns(i["final_w_2"]),
    }
    for name, n in VEC_PARTS:
        assert parts[name].shape == (P, n), (name, parts[name].shape)
    arrays["vec"] = np.concatenate([parts[name] for name, _ in VEC_PARTS], axis=1)
    arrays.update(second_layouts(i))
    return {k: np.ascontiguousarray(a) for k, a in arrays.items()}


def second_layouts(i):
    rw, ml = i["rw_w_in_2"][0], i["ml_w_in_2"][0]
    big = np.concatenate([rw[:, 0:D], rw[:, D + 64:3 * D + 64]], axis=1)
    small = np.concatenate([rw[:, D:D + 64], rw[:, 3 * D + 64:]], axis=1)
    gu = [tiles(w).reshape(2, FF_TILES, P, KT, P).transpose(1, 0, 2, 3, 4).reshape(2 * FF_TILES, P, KT, P)
          for w in i["ffn_w_gu_2"]]
    return {
        "w_rw": tiles(big),
        "w_rw_small": small.reshape(KT, P, 288).transpose(1, 0, 2),
        "w2": i["rw_w2_2"][0].reshape(64, KT, P).transpose(1, 0, 2),
        "a2": i["rw_a2_2"][0].reshape(64, KT, P).transpose(1, 0, 2),
        "g2": i["rw_g2_2"][0].reshape(160, KT, P).transpose(1, 0, 2),
        "w_rw_out": tiles(i["rw_w_out_2"][0]),
        "w_ml": tiles(ml[:, :3 * D]),
        "w_ml_gates": ml[:, 3 * D:].reshape(KT, P, 16).transpose(1, 0, 2),
        "w_ml_out": tiles(i["ml_w_out_2"][0]),
        "w_gu": np.concatenate(gu),
        "w_down": np.concatenate([tiles(w) for w in i["ffn_w_down_2"]]),
    }


def kernel(**inputs):
    import concourse.bacc as bacc
    from concourse.bass_utils import run_bass_kernel_spmd

    arrays = layouts(inputs)
    nc = bacc.Bacc("TRN2", target_bir_lowering=False, num_devices=1)
    io = {k: nc.dram_tensor(f"in_{k}", a.shape, mybir.dt.from_np(a.dtype), kind="ExternalInput").ap()
          for k, a in arrays.items()}
    io["out"] = nc.dram_tensor("out_x", (P, KT, S), F32, kind="ExternalOutput").ap()
    for name, shape in SCRATCH.items():
        io[name] = nc.dram_tensor(name, shape, F32).ap()
    build(nc, io)
    r = run_bass_kernel_spmd(nc, [{f"in_{k}": a for k, a in arrays.items()}], core_ids=[0])
    got = r.results[0]["out_x"]
    return np.ascontiguousarray(got.transpose(1, 0, 2).reshape(D, S).T)[None]
```
